# Optimizing a Trainium2 kernel written in Bass

```python
import math
import jax, jax.numpy as jnp
from jax import lax
import numpy as np

D_MODEL = 1024
BATCH = 1
SEQ = 2048
DEPTH = 1

GRID_W = 64
CTX_LEN = 256
D_HG = 512
HG_HEADS = 4
HG_DK = D_HG // HG_HEADS
HG_DV = HG_DK
HG_CHUNK = 64
D_RW = D_MODEL - D_HG
RW_HEAD = 64
RW_HEADS = D_RW // RW_HEAD
RW_DECAY_LORA = 32
RW_AAA_LORA = 32
RW_GATE_LORA = 96
HG_COLS = 5 * D_HG
RW_COLS = 3 * D_RW + 2 * RW_DECAY_LORA + RW_AAA_LORA + RW_GATE_LORA
D_IN = HG_COLS + RW_COLS
N_GROUPS = 8
EXPERTS_PER_GROUP = 8
N_EXPERTS = N_GROUPS * EXPERTS_PER_GROUP
TOP_K_INNER = 2
D_EXPERT = 512
MOE_BLOCK = 128
N_MOD = 6
DN_ALPHA = (2.0 * DEPTH) ** 0.25
DN_BETA = (8.0 * DEPTH) ** -0.25
LN_EPS = 1e-5
HEAD_NORM_EPS = 1e-6
RW_GN_EPS = 64e-5
RW_DECAY_SCALE = math.exp(-0.5)

kernel_name = "hybrid_hgrn2_rwkv7_hmoe_dit_block"

def layer_norm(x):
    xf = x.astype(jnp.float32)
    mu = jnp.mean(xf, -1, keepdims=True)
    var = jnp.mean(jnp.square(xf - mu), -1, keepdims=True)
    return ((xf - mu) * lax.rsqrt(var + LN_EPS)).astype(x.dtype)

def ln_affine(x, g, b):
    return layer_norm(x) * g + b

def dir_stack(fwd, bwd):
    return jnp.stack([fwd, jnp.flip(bwd, axis=1)])

def dir_merge(o):
    return o[0] + jnp.flip(o[1], axis=1)

def grid_shift(p, rows):
    b, l, ch = p.shape
    g = p.reshape(b, rows, GRID_W, ch)
    gp = jnp.pad(g, ((0, 0), (1, 1), (1, 1), (0, 0)))
    nb = 0.25 * (gp[:, :-2, 1:-1] + gp[:, 2:, 1:-1] + gp[:, 1:-1, :-2] + gp[:, 1:-1, 2:])
    return nb.reshape(b, l, ch)

def seq_shift(p):
    pp = jnp.pad(p, ((0, 0), (1, 1), (0, 0)))
    return 0.5 * (pp[:, :-2] + pp[:, 2:])

def hg_heads(t):
    return t.reshape(t.shape[:-1] + (HG_HEADS, HG_DK))

def rw_heads(t):
    return t.reshape(t.shape[:-1] + (RW_HEADS, RW_HEAD))

def hgrn2_prep(p, lb):
    q, i, zf, zb, g = jnp.split(p.astype(jnp.float32), 5, axis=-1)
    z = dir_stack(zf, zb)
    lbb = lb[:, None, None, :]
    logf = jnp.logaddexp(jnp.log(lbb), jnp.log1p(-lbb) + jax.nn.log_sigmoid(z))
    k = (1.0 - lbb) * jax.nn.sigmoid(-z)
    qs = jax.nn.silu(q)
    return hg_heads(dir_stack(qs, qs)), hg_heads(k), hg_heads(dir_stack(i, i)), hg_heads(logf), g

def hgrn2_chunk_scan(q, k, v, logf, s0):
    n, b, l, h, _ = q.shape
    nc = l // HG_CHUNK

    def to_chunks(t):
        return t.reshape(n, b, nc, HG_CHUNK, h, t.shape[-1]).transpose(2, 0, 1, 4, 3, 5)

    xs = tuple(to_chunks(t) for t in (q, k, v, logf))
    causal = jnp.tril(jnp.ones((HG_CHUNK, HG_CHUNK), bool))[:, :, None]

    def step(s, inp):
        qq, kk, vv, ff = inp
        bc = jnp.cumsum(ff, axis=-2)
        o_inter = jnp.einsum('nbhcd,nbhde->nbhce', qq * jnp.exp(bc), s)
        diff = bc[..., :, None, :] - bc[..., None, :, :]
        decay = jnp.where(causal, jnp.exp(jnp.where(causal, diff, 0.0)), 0.0)
        scores = jnp.einsum('nbhtd,nbhsd,nbhtsd->nbhts', qq, kk, decay)
        o = o_inter + jnp.einsum('nbhts,nbhse->nbhte', scores, vv)
        blast = bc[..., -1:, :]
        s_new = jnp.exp(blast[..., 0, :])[..., None] * s + jnp.einsum(
            'nbhsd,nbhse->nbhde', kk * jnp.exp(blast - bc), vv)
        return s_new, o

    s_fin, o = lax.scan(step, s0, xs)
    o = o.transpose(1, 2, 0, 4, 3, 5).reshape(n, b, l, h, HG_DV)
    return o, s_fin

def hgrn2_readout(o, g, norm_w):
    o = dir_merge(o)
    o = o * lax.rsqrt(jnp.mean(o * o, -1, keepdims=True) + HEAD_NORM_EPS)
    o = o.reshape(o.shape[:-2] + (D_HG,)) * norm_w
    return o * jax.nn.silu(g)

def rwkv7_prep(p, p_nb, mu, w0, w_decay2, a0, w_a2, w_g2, k_k, k_a):
    p = p.astype(jnp.float32)
    p = p + (p_nb.astype(jnp.float32) - p) * mu
    cuts = [D_RW, 2 * D_RW, 3 * D_RW, 3 * D_RW + RW_DECAY_LORA, 3 * D_RW + 2 * RW_DECAY_LORA,
            3 * D_RW + 2 * RW_DECAY_LORA + RW_AAA_LORA]
    r, k, v, lwf, lwb, la, lg = jnp.split(p, cuts, axis=-1)
    w_logit = dir_stack(w0[0] + jnp.tanh(lwf) @ w_decay2[0], w0[1] + jnp.tanh(lwb) @ w_decay2[1])
    decay = jnp.exp(-RW_DECAY_SCALE * jax.nn.sigmoid(w_logit))
    a = jax.nn.sigmoid(a0 + la @ w_a2)
    g = jax.nn.sigmoid(lg) @ w_g2
    kk = rw_heads(k * k_k)
    kk = kk * lax.rsqrt(jnp.maximum(jnp.sum(kk * kk, -1, keepdims=True), 1e-12))
    k = rw_heads(k * (1.0 + (a - 1.0) * k_a))
    r, v, a = rw_heads(r), rw_heads(v), rw_heads(a)
    scan_in = (dir_stack(r, r), rw_heads(decay), dir_stack(k, k), dir_stack(v, v),
               dir_stack(kk, kk), dir_stack(a, a))
    return scan_in, (r, k, v, g)

def rwkv7_scan(r, w, k, v, kk, a, s0):
    def step(s, inp):
        rt, wt, kt, vt, kkt, at = inp
        sa = jnp.einsum('nbhij,nbhj->nbhi', s, kkt)
        s = (s * wt[..., None, :] - sa[..., :, None] * (kkt * at)[..., None, :]
             + vt[..., :, None] * kt[..., None, :])
        return s, jnp.einsum('nbhij,nbhj->nbhi', s, rt)

    xs = tuple(jnp.moveaxis(t, 2, 0) for t in (r, w, k, v, kk, a))
    s_fin, y = lax.scan(step, s0, xs)
    return jnp.moveaxis(y, 0, 2), s_fin

def rwkv7_readout(y, r, k, v, g, r_k, gn_w, gn_b):
    y = dir_merge(y)
    mu = jnp.mean(y, -1, keepdims=True)
    var = jnp.mean(jnp.square(y - mu), -1, keepdims=True)
    yn = ((y - mu) * lax.rsqrt(var + RW_GN_EPS)).reshape(y.shape[:-2] + (D_RW,)) * gn_w + gn_b
    bonus = jnp.sum(r * k * r_k, -1, keepdims=True) * v
    return (yn + bonus.reshape(bonus.shape[:-2] + (D_RW,))) * g

def token_mixer(h, hc, rows, lb, w_in, w_out, hg_norm_w, rw_mu, rw_w0, rw_w_decay2, rw_a0, rw_w_a2,
                rw_w_g2, rw_k_k, rw_k_a, rw_r_k, rw_gn_w, rw_gn_b, need_ctx):
    b = h.shape[0]
    p = h @ w_in
    pc = hc @ w_in
    q_c, k_c, v_c, f_c, g_c = hgrn2_prep(pc[..., :HG_COLS], lb)
    q_l, k_l, v_l, f_l, g_l = hgrn2_prep(p[..., :HG_COLS], lb)
    s0 = jnp.zeros((2, b, HG_HEADS, HG_DK, HG_DV), jnp.float32)
    o_c, s_c = hgrn2_chunk_scan(q_c, k_c, v_c, f_c, s0)
    o_l, _ = hgrn2_chunk_scan(q_l, k_l, v_l, f_l, s_c)
    rw_prm = (rw_mu, rw_w0, rw_w_decay2, rw_a0, rw_w_a2, rw_w_g2, rw_k_k, rw_k_a)
    rc = pc[..., HG_COLS:]
    rl = p[..., HG_COLS:]
    sin_c, aux_c = rwkv7_prep(rc, seq_shift(rc), *rw_prm)
    sin_l, aux_l = rwkv7_prep(rl, grid_shift(rl, rows), *rw_prm)
    st0 = jnp.zeros((2, b, RW_HEADS, RW_HEAD, RW_HEAD), jnp.float32)
    y_c, st_c = rwkv7_scan(*sin_c, st0)
    y_l, _ = rwkv7_scan(*sin_l, st_c)
    out_l = jnp.concatenate([hgrn2_readout(o_l, g_l, hg_norm_w),
                             rwkv7_readout(y_l, *aux_l, rw_r_k, rw_gn_w, rw_gn_b)], -1) @ w_out
    out_c = None
    if need_ctx:
        out_c = (jnp.concatenate([hgrn2_readout(o_c, g_c, hg_norm_w),
                                  rwkv7_readout(y_c, *aux_c, rw_r_k, rw_gn_w, rw_gn_b)], -1) @ w_out
                 ).astype(hc.dtype)
    return out_l.astype(h.dtype), out_c

def hier_moe(h, w_group, b_group, w_router, b_router, w_gate, w_up, w_down):
    b, l, d = h.shape
    t = h.reshape(-1, d)
    n_tok = t.shape[0]
    gl = (t @ w_group + b_group).astype(jnp.float32)
    g_idx = jnp.argmax(gl, -1)
    g_prob = jnp.take_along_axis(jax.nn.softmax(gl, -1), g_idx[:, None], -1)
    el = (t @ w_router).reshape(n_tok, N_GROUPS, EXPERTS_PER_GROUP) + b_router
    el = jnp.take_along_axis(el, g_idx[:, None, None], 1)[:, 0].astype(jnp.float32)
    top_v, top_i = lax.top_k(el, TOP_K_INNER)
    wts = jax.nn.softmax(top_v, -1) * g_prob
    e_idx = g_idx[:, None].astype(jnp.int32) * EXPERTS_PER_GROUP + top_i.astype(jnp.int32)
    n_as = n_tok * TOP_K_INNER
    flat_e = e_idx.reshape(-1)
    flat_tok = jnp.repeat(jnp.arange(n_tok, dtype=jnp.int32), TOP_K_INNER)
    flat_w = wts.reshape(-1)
    order = jnp.argsort(flat_e)
    se = flat_e[order]
    counts = jnp.bincount(flat_e, length=N_EXPERTS)
    starts = jnp.cumsum(counts) - counts
    padded = (counts + MOE_BLOCK - 1) // MOE_BLOCK * MOE_BLOCK
    pad_ends = jnp.cumsum(padded)
    pad_starts = pad_ends - padded
    dest = pad_starts[se] + (jnp.arange(n_as) - starts[se])
    n_blocks = -(-n_as // MOE_BLOCK) + N_EXPERTS
    cap = n_blocks * MOE_BLOCK
    row_tok = jnp.full((cap,), n_tok, jnp.int32).at[dest].set(flat_tok[order])
    row_w = jnp.zeros((cap,), jnp.float32).at[dest].set(flat_w[order])
    block_exp = jnp.minimum(
        jnp.searchsorted(pad_ends, jnp.arange(n_blocks) * MOE_BLOCK, side='right'), N_EXPERTS - 1)
    t_pad = jnp.concatenate([t, jnp.zeros((1, d), t.dtype)], 0)
    xb = t_pad[row_tok].reshape(n_blocks, MOE_BLOCK, d)

    def expert_block(args):
        xblk, e = args
        hid = jax.nn.silu(xblk @ w_gate[e]) * (xblk @ w_up[e])
        return hid @ w_down[e]

    yb = lax.map(expert_block, (xb, block_exp))
    y = jax.ops.segment_sum(yb.reshape(cap, d).astype(jnp.float32) * row_w[:, None], row_tok,
                            num_segments=n_tok + 1)[:n_tok]
    return y.reshape(b, l, d).astype(h.dtype)

def setup_inputs(seed: int = 0) -> dict:
    key = jax.random.key(seed)
    ks = iter(jax.random.split(key, 40))
    D = D_MODEL

    def nrm(shape, scale):
        return jax.random.normal(next(ks), shape, jnp.float32) * scale

    def uni(shape):
        return jax.random.uniform(next(ks), shape, jnp.float32)

    return {
        "x": nrm((BATCH, SEQ, D), 1.0),
        "c": nrm((BATCH, D), 1.0),
        "ctx": nrm((BATCH, CTX_LEN, D), 1.0),
        "c_ctx": nrm((D,), 1.0),
        "w_mod": nrm((DEPTH, D, N_MOD * D), D ** -0.5),
        "b_mod": nrm((DEPTH, N_MOD * D), 0.02),
        "w_in": nrm((DEPTH, D, D_IN), D ** -0.5),
        "w_out": nrm((DEPTH, D, D), D ** -0.5 * DN_BETA),
        "hg_lb_logits": nrm((2, DEPTH + 1, D_HG), 0.5),
        "hg_norm_w": 1.0 + nrm((DEPTH, D_HG), 0.05),
        "rw_mu": uni((DEPTH, RW_COLS)),
        "rw_w0": nrm((DEPTH, 2, D_RW), 0.5) - 0.5,
        "rw_w_decay2": nrm((DEPTH, 2, RW_DECAY_LORA, D_RW), 0.1),
        "rw_a0": nrm((DEPTH, D_RW), 0.1),
        "rw_w_a2": nrm((DEPTH, RW_AAA_LORA, D_RW), 0.1),
        "rw_w_g2": nrm((DEPTH, RW_GATE_LORA, D_RW), RW_GATE_LORA ** -0.5),
        "rw_k_k": 0.85 + nrm((DEPTH, D_RW), 0.05),
        "rw_k_a": 1.0 + nrm((DEPTH, D_RW), 0.05),
        "rw_r_k": nrm((DEPTH, RW_HEADS, RW_HEAD), 0.1),
        "rw_gn_w": 1.0 + nrm((DEPTH, D_RW), 0.05),
        "rw_gn_b": nrm((DEPTH, D_RW), 0.02),
        "ln1_g": 1.0 + nrm((DEPTH, D), 0.05),
        "ln1_b": nrm((DEPTH, D), 0.02),
        "ln2_g": 1.0 + nrm((DEPTH, D), 0.05),
        "ln2_b": nrm((DEPTH, D), 0.02),
        "moe_w_group": nrm((DEPTH, D, N_GROUPS), D ** -0.5),
        "moe_b_group": nrm((DEPTH, N_GROUPS), 0.01),
        "moe_w_router": nrm((DEPTH, D, N_EXPERTS), D ** -0.5),
        "moe_b_router": nrm((DEPTH, N_GROUPS, EXPERTS_PER_GROUP), 0.01),
        "moe_w_gate": nrm((DEPTH, N_EXPERTS, D, D_EXPERT), D ** -0.5),
        "moe_w_up": nrm((DEPTH, N_EXPERTS, D, D_EXPERT), D ** -0.5),
        "moe_w_down": nrm((DEPTH, N_EXPERTS, D_EXPERT, D), D_EXPERT ** -0.5 * DN_BETA),
    }

def reference(x, c, ctx, c_ctx, w_mod, b_mod, w_in, w_out, hg_lb_logits, hg_norm_w, rw_mu, rw_w0,
              rw_w_decay2, rw_a0, rw_w_a2, rw_w_g2, rw_k_k, rw_k_a, rw_r_k, rw_gn_w, rw_gn_b,
              ln1_g, ln1_b, ln2_g, ln2_b, moe_w_group, moe_b_group, moe_w_router, moe_b_router,
              moe_w_gate, moe_w_up, moe_w_down):
    rows = x.shape[1] // GRID_W
    lb_all = jnp.cumsum(jax.nn.softmax(hg_lb_logits.astype(jnp.float32), axis=1), axis=1)
    for l in range(DEPTH):
        need_ctx = l < DEPTH - 1
        mod = jax.nn.silu(c) @ w_mod[l] + b_mod[l]
        sh1, sc1, g1, sh2, sc2, g2 = jnp.split(mod[:, None, :], N_MOD, axis=-1)
        modc = jax.nn.silu(c_ctx) @ w_mod[l] + b_mod[l]
        csh1, csc1, cg1, csh2, csc2, cg2 = jnp.split(modc, N_MOD, axis=-1)
        h = layer_norm(x) * (1.0 + sc1) + sh1
        hc = layer_norm(ctx) * (1.0 + csc1) + csh1
        y, yc = token_mixer(h, hc, rows, lb_all[:, l], w_in[l], w_out[l], hg_norm_w[l], rw_mu[l],
                            rw_w0[l], rw_w_decay2[l], rw_a0[l], rw_w_a2[l], rw_w_g2[l], rw_k_k[l],
                            rw_k_a[l], rw_r_k[l], rw_gn_w[l], rw_gn_b[l], need_ctx)
        x = ln_affine(DN_ALPHA * x + g1 * y, ln1_g[l], ln1_b[l])
        h2 = layer_norm(x) * (1.0 + sc2) + sh2
        x = ln_affine(DN_ALPHA * x + g2 * hier_moe(h2, moe_w_group[l], moe_b_group[l], moe_w_router[l],
                                                     moe_b_router[l], moe_w_gate[l], moe_w_up[l],
                                                     moe_w_down[l]), ln2_g[l], ln2_b[l])
        if need_ctx:
            ctx = ln_affine(DN_ALPHA * ctx + cg1 * yc, ln1_g[l], ln1_b[l])
            hc2 = layer_norm(ctx) * (1.0 + csc2) + csh2
            ctx = ln_affine(DN_ALPHA * ctx + cg2 * hier_moe(hc2, moe_w_group[l], moe_b_group[l],
                                                             moe_w_router[l], moe_b_router[l],
                                                             moe_w_gate[l], moe_w_up[l], moe_w_down[l]),
                            ln2_g[l], ln2_b[l])
    return x


_drawn_inputs = setup_inputs


def setup_inputs(seed=0):
    import zlib

    import numpy as np

    out = dict(_drawn_inputs(seed))
    spreads = {}
    factors = {'ctx': 8.0,
     'c_ctx': 8.0,
     'hg_lb_logits': 6.902,
     'hg_norm_w': 3.881,
     'rw_w_decay2': 2.91,
     'rw_a0': 5.165,
     'rw_k_k': 4.841,
     'rw_k_a': 3.541,
     'rw_gn_w': 5.917,
     'rw_gn_b': 23.594,
     'ln2_b': 2.85,
     'moe_b_group': 22.823,
     'moe_b_router': 21.802}
    for name, (base, spread) in spreads.items():
        noise = np.random.default_rng([zlib.crc32(name.encode()), seed]).standard_normal(out[name].shape)
        drawn = base * np.exp(spread * noise) if base else spread * noise
        out[name] = __import__('jax').numpy.asarray(drawn.astype(out[name].dtype))
    for name, factor in factors.items():
        out[name] = (out[name] * factor).astype(out[name].dtype)
    return out
```

```python
import math
from contextlib import ExitStack

import concourse.bass as bass
from concourse import mybir

F32 = mybir.dt.float32
I32 = mybir.dt.int32
U32 = mybir.dt.uint32
ALU = mybir.AluOpType
ACT = mybir.ActivationFunctionType
AX = mybir.AxisListType

P = 128
D = 1024
KD = D // P
LAT = 2048
CTX = 256
GRID_W = 64
GROUP = 256
NG = (CTX + LAT) // GROUP
D_HG = 512
HH = 4
D_RW = 512
RH = 8
NPAIR = 4
LORA = 32
GATE_LORA = 96
D_IN = 5 * D_HG + 3 * D_RW + 3 * LORA + GATE_LORA
HG_STEPS = (CTX + LAT) // 128
RW_C = 64
RW_STEPS = (CTX + LAT) // RW_C
N_EXP = 64
N_GRP = 8
D_EXP = 512
BLK = 128
N_TILES = LAT // P
MAX_BLOCKS = 2 * LAT // BLK + N_EXP
ALPHA = 2.0 ** 0.25
LN_EPS = 1e-5
HEAD_EPS = 1e-6
GN_EPS = 64e-5
DECAY = math.exp(-0.5)


class Order:

    def __init__(self, eng, sem):
        self.eng, self.sem, self.per, self.g, self.k = eng, sem, 0, 0, 0

    def count(self, ins):
        self.k += 1
        ins.then_inc(self.sem, 1)

    def link(self, ins):
        self.count(ins)
        self.eng.wait_ge(self.sem, self.g * self.per + self.k)

    def repeat(self, first, count, body):
        self.g, self.k = 0, 0
        base = self.k
        body(0)
        self.per = self.k
        if count > 1:
            with self.eng.Fori(1, count) as g:
                self.g, self.k = g, 0
                body(g)
                assert self.k == self.per


def peel(eng, count, body):
    body(0)
    if count > 1:
        with eng.Fori(1, count) as g:
            body(g)


class Mem:

    def __init__(self, nc, ctx, stage):
        self.nc, self.ctx, self.stage, self.sems = nc, ctx, stage, []
        ctx.callback(self.release)

    def sb(self, name, shape, dt=F32):
        return self.ctx.enter_context(self.nc.sbuf_tensor(f"{self.stage}_{name}", shape, dt))

    def ps(self, name, shape, dt=F32):
        return self.ctx.enter_context(self.nc.psum_tensor(f"{self.stage}_{name}", shape, dt))

    def sem(self, name):
        self.sems.append(self.nc.alloc_semaphore(f"{self.stage}_{name}"))
        return self.sems[-1]

    def release(self):
        self.nc.clear_and_free_semaphores(self.sems)
        self.nc.all_engine_barrier()


def modulation(nc, A, S, K):
    with ExitStack() as ctx:
        m = Mem(nc, ctx, "mod")
        HALF = 6 * D // 2
        cols = m.sb("c_cols", [P, 2, KD])
        sg = m.sb("c_sig", [P, 2, KD])
        cs = m.sb("c_silu", [P, KD, 2])
        w = m.sb("w", [P, 4, HALF])
        bias = m.sb("bias", [2, 6 * D])
        row = m.sb("row", [2, 6 * D])
        lbl = m.sb("lb_logits", [P, 2, 2, HH])
        lmax = m.sb("lb_max", [P, 2, HH])
        lexp = m.sb("lb_exp", [P, 2, 2, HH])
        lsum = m.sb("lb_sum", [P, 2, HH])
        zeros = m.sb("zeros", [P, 14 * GRID_W])
        acc = [m.ps(f"acc{j}", [P, 512]) for j in range(6)]
        in_sem, w_sem = m.sem("inputs_loaded"), [m.sem(f"w_loaded{j}") for j in range(4)]
        sig_sem, silu_sem, ev_sem, out_sem = (m.sem(x) for x in ("sigmoid_done", "silu_done", "half_added", "rows_stored"))
        k_sem = m.sem("k_tile_used")
        lb_sem, lexp_sem, vo, z_sem = m.sem("lb_max_done"), m.sem("lb_exp_done"), m.sem("dve_order"), m.sem("zeros_set")
        po, l_sem = m.sem("pool_order"), m.sem("spare_rows_set")
        spare = m.sb("spare_rows", [P, MAX_BLOCKS + 2, 2], I32)

        with nc.Block() as block:
            @block.sync
            def _(sp):
                sp.dma_start(cols[:, 0, :], A["c"].rearrange("a (k p) -> p (a k)", p=P)).then_inc(in_sem, 16)
                sp.dma_start(cols[:, 1, :], A["c_ctx"].rearrange("(k p) -> p k", p=P)).then_inc(in_sem, 16)
                for r in range(2):
                    sp.dma_start(bias[r:r + 1, :], A["b_mod"]).then_inc(in_sem, 16)
                for d in range(2):
                    for l in range(2):
                        sp.dma_start(lbl[:, d, l, :], A["hg_lb_logits"][d, l].rearrange("(h p) -> p h", p=P)).then_inc(in_sem, 16)
                for t in range(16):
                    half, k = t // 8, t % 8
                    if t >= 4:
                        sp.wait_ge(k_sem, t - 3)
                    sp.dma_start(w[:, t % 4, :], A["w_mod"][0, k * P:(k + 1) * P, half * HALF:(half + 1) * HALF]).then_inc(w_sem[t % 4], 16)
                sp.wait_ge(z_sem, 1)
                zv = zeros[:].rearrange("p (t w) -> p t w", t=14)
                sp.dma_start(S["rw_lat"][:, :, 0:GRID_W].rearrange("t p w -> p t w"), zv).then_inc(out_sem, 16)
                sp.dma_start(S["rw_lat"][:, :, GRID_W + LAT:].rearrange("t p w -> p t w"), zv).then_inc(out_sem, 16)
                sp.dma_start(S["rw_ctx"][:, :, 0:1].rearrange("t p w -> p t w"), zv[:, :, 0:1]).then_inc(out_sem, 16)
                sp.dma_start(S["rw_ctx"][:, :, CTX + 1:].rearrange("t p w -> p t w"), zv[:, :, 0:1]).then_inc(out_sem, 16)
                sp.wait_ge(l_sem, 1)
                sp.dma_start(S["row_list"].rearrange("(p a) o -> p a o", p=P), spare[:]).then_inc(out_sem, 16)
                sp.wait_ge(ev_sem, 12)
                sp.dma_start(S["mod"], row[:]).then_inc(out_sem, 16)
                sp.wait_ge(out_sem, 16 * 6)

            @block.gpsimd
            def _(pool):
                nc.gpsimd.memset(zeros[:], 0.0).then_inc(z_sem, 1)
                nc.gpsimd.memset(spare[:, :, 0:1], 0)
                nc.gpsimd.memset(spare[:, :, 1:2], 2 * LAT).then_inc(l_sem, 1)
                nc.gpsimd.memset(K["half"][:], -0.5)
                nc.gpsimd.memset(K["ones"][:], 1.0)
                nc.gpsimd.memset(K["ident"][:], 0.0).then_inc(po, 1)
                pool.wait_ge(po, 1)
                nc.gpsimd.affine_select(out=K["ident"][:], in_=K["ident"][:], compare_op=ALU.not_equal, fill=1.0,
                                        base=0, pattern=[[-1, P]], channel_multiplier=1)

            @block.scalar
            def _(act):
                act.wait_ge(in_sem, 16 * 8)
                nc.scalar.activation(sg[:], cols[:], ACT.Sigmoid).then_inc(sig_sem, 1)
                act.wait_ge(lb_sem, 1)
                nc.scalar.activation(lexp[:], lbl[:], ACT.Exp).then_inc(lexp_sem, 1)

            @block.vector
            def _(dve):
                o = Order(dve, vo)
                dve.wait_ge(in_sem, 16 * 8)
                o.link(nc.vector.tensor_tensor(lmax[:], lbl[:, :, 0, :], lbl[:, :, 1, :], ALU.max))
                o.link(nc.vector.tensor_tensor(lbl[:, :, 0, :], lbl[:, :, 0, :], lmax[:], ALU.subtract))
                nc.vector.tensor_tensor(lbl[:, :, 1, :], lbl[:, :, 1, :], lmax[:], ALU.subtract).then_inc(lb_sem, 1)
                dve.wait_ge(sig_sem, 1)
                nc.vector.tensor_tensor(cs[:].rearrange("p k r -> p r k"), cols[:], sg[:], ALU.mult).then_inc(silu_sem, 1)
                dve.wait_ge(lexp_sem, 1)
                o.link(nc.vector.tensor_tensor(lsum[:], lexp[:, :, 0, :], lexp[:, :, 1, :], ALU.add))
                o.link(nc.vector.reciprocal(lsum[:], lsum[:]))
                nc.vector.tensor_tensor(K["lb"][:], lexp[:, :, 0, :], lsum[:], ALU.mult)
                nc.vector.tensor_tensor(K["omlb"][:], lexp[:, :, 1, :], lsum[:], ALU.mult)
                for half in range(2):
                    dve.wait_ge(k_sem, 8 * half + 8)
                    for j in range(6):
                        c0 = half * HALF + j * 512
                        nc.vector.tensor_tensor(row[:, c0:c0 + 512], acc[j][0:2, :], bias[:, c0:c0 + 512], ALU.add).then_inc(ev_sem, 1)

            @block.tensor
            def _(pe):
                pe.wait_ge(silu_sem, 1)
                for t in range(16):
                    half, k = t // 8, t % 8
                    pe.wait_ge(w_sem[t % 4], 16 * (t // 4 + 1))
                    if t == 8:
                        pe.wait_ge(ev_sem, 6)
                    for j in range(6):
                        mm = nc.tensor.matmul(acc[j][0:2, :], cs[:, k, :], w[:, t % 4, j * 512:(j + 1) * 512],
                                              start=(k == 0), stop=(k == 7))
                    mm.then_inc(k_sem, 1)


def projection(nc, A, S, K):
    with ExitStack() as ctx:
        m = Mem(nc, ctx, "proj")
        w_in = m.sb("w_in", [P, KD, D_IN])
        x = m.sb("x", [P, 2, D])
        stats = m.sb("stats", [P, 2, 2, 6])
        mv = m.sb("mean_var", [P, 2, 2])
        rstd = m.sb("rstd", [P, 2])
        hT = m.sb("hT", [P, KD, GROUP])
        cols = m.sb("mod_cols", [P, 2, 2, KD])
        sig = m.sb("sig", [P, 2, 2, GROUP])
        sigg = m.sb("sig_gate", [P, D_HG])
        qo = m.sb("q_out", [P, HH, GROUP])
        ko = m.sb("k_out", [P, 2, HH, GROUP])
        fo = m.sb("f_out", [P, 2, HH, GROUP])
        ro = m.sb("rw_out", [P, 14, GROUP])
        io = m.sb("i_out", [P, 2, D_HG])
        go = m.sb("g_out", [P, 2, D_HG])
        tp = [m.ps(f"turned{j}", [P, 512]) for j in range(4)]
        mp = [m.ps(f"product{j}", [P, 512]) for j in range(3)]
        names = ("w_loaded x_loaded normed rstd_ready stats_ready turned hT_ready_act hT_ready_dve product_done product_free "
                 "sig_ready sig_used q_ready q_stored k_ready z_stored rw_ready rw_stored i_ready i_stored g_ready "
                 "g_stored dve_order cols_loaded cols_ready z_sig sigg_ready")
        s = {n: m.sem(n) for n in names.split()}

        outs = [("q", h, h * P, P) for h in range(HH)]
        outs += [("z", 4 * d + h, 2 * D_HG + d * D_HG + h * P, P) for d in range(2) for h in range(HH)]
        outs += [("rw", j, 5 * D_HG + j * P, P) for j in range(12)]
        outs += [("rw", 12, 5 * D_HG + 12 * P, GATE_LORA), ("rw", 13, 5 * D_HG + 12 * P + GATE_LORA, GATE_LORA)]
        outs += [("i", u, D_HG, D_HG) for u in range(2)] + [("g", u, 4 * D_HG, D_HG) for u in range(2)]
        NO = len(outs)
        assert NO % 3 == 0
        N_SIG = 4 + 2 * 8 + 2

        with nc.Block() as block:
            @block.sync
            def _(sp):
                for r, (src, c0) in enumerate(((1, 0), (0, 0))):
                    for j in range(2):
                        sp.dma_start(cols[:, r, j, :], S["mod"][src, (c0 + j) * D:(c0 + j + 1) * D].rearrange("(k p) -> p k", p=P)).then_inc(s["cols_loaded"], 16)
                for u in range(2):
                    sp.dma_start(x[:, u, :], A["ctx"][0, u * P:(u + 1) * P, :]).then_inc(s["x_loaded"], 16)
                for k in range(KD):
                    sp.dma_start(w_in[:, k, :], A["w_in"][0, k * P:(k + 1) * P, :]).then_inc(s["w_loaded"], 16)

                def body(g):
                    sp.wait_ge(s["turned"], 4 * g + 4)
                    for u in range(2):
                        sp.dma_start(x[:, u, :], A["x"][0, bass.ds(g * GROUP + u * P, P), :]).then_inc(s["x_loaded"], 16)
                peel(sp, NG - 1, body)

            @block.gpsimd
            def _(pool):
                def norm(g):
                    for u in range(2):
                        pool.wait_ge(s["stats_ready"], 2 * g + u + 1)
                        nc.gpsimd.tensor_tensor(rstd[:, u:u + 1], mv[:, u, 1:2], K["half"][:, 0:1], ALU.pow).then_inc(s["rstd_ready"], 1)

                def stores(g, ctx_group):
                    q0 = 2 * g
                    back = (lambda c: 1 - c) if ctx_group else (lambda c: (HG_STEPS + 1 - c) - 2 * g)
                    pool.wait_ge(s["q_ready"], 4 * g + 4)
                    for c in range(2):
                        for d, n in ((0, q0 + c), (1, back(c))):
                            pool.dma_start(S["hg_in"][d, bass.ds(n, 1), 0].rearrange("n p h t -> p (n h) t"),
                                           qo[:, :, c * P:(c + 1) * P]).then_inc(s["q_stored"], 16)
                    for d in range(2):
                        pool.wait_ge(s["k_ready"], 8 * g + 4 * d + 4)
                        for c in range(2):
                            n = q0 + c if d == 0 else back(c)
                            for j, buf in ((1, ko), (2, fo)):
                                pool.dma_start(S["hg_in"][d, bass.ds(n, 1), j].rearrange("n p h t -> p (n h) t"),
                                               buf[:, d, :, c * P:(c + 1) * P]).then_inc(s["z_stored"], 16)
                    pool.wait_ge(s["rw_ready"], 14 * g + 14)
                    for lo, hi, rows in ((0, 12, P), (12, 14, GATE_LORA)):
                        dst = S["rw_ctx"] if ctx_group else S["rw_lat"]
                        off = 1 if ctx_group else g * GROUP - GROUP + GRID_W
                        pool.dma_start(dst[lo:hi, 0:rows, bass.ds(off, GROUP)].rearrange("t p c -> p t c"),
                                       ro[0:rows, lo:hi, :]).then_inc(s["rw_stored"], 16)
                    pool.wait_ge(s["i_ready"], 2 * g + 2)
                    for c in range(2):
                        for d, n in ((0, q0 + c), (1, back(c))):
                            pool.dma_start(S["hg_v"][d, bass.ds(n, 1)].rearrange("n p e -> p (n e)"), io[:, c, :]).then_inc(s["i_stored"], 16)
                    pool.wait_ge(s["g_ready"], 2 * g + 2)
                    for c in range(2):
                        pool.dma_start(S["hg_g"][bass.ds(g * GROUP + c * P, P), :], go[:, c, :]).then_inc(s["g_stored"], 16)

                norm(0)
                norm(1)
                stores(0, True)
                with pool.Fori(1, NG - 1) as g:
                    norm(g + 1)
                    stores(g, False)
                stores(NG - 1, False)
                for n, per in (("q_stored", 4), ("z_stored", 8), ("rw_stored", 2), ("i_stored", 4), ("g_stored", 2)):
                    pool.wait_ge(s[n], 16 * per * NG)

            @block.scalar
            def _(act):
                def turn(g, row):
                    act.wait_ge(s["cols_ready"], 1)
                    for k in range(KD):
                        if k % 4 == 0:
                            act.wait_ge(s["turned"], 4 * g + k // 4 + 1)
                        nc.scalar.activation(hT[:, k, 0:P], tp[k // 4][:, (k % 4) * P:(k % 4 + 1) * P], ACT.Identity,
                                             bias=cols[:, row, 0, k:k + 1], scale=cols[:, row, 1, k:k + 1]).then_inc(s["hT_ready_act"], 1)

                def outputs(g):
                    sg = 0
                    for o, (kind, j, _, width) in enumerate(outs):
                        p = mp[o % 3]
                        if kind in "qzg":
                            act.wait_ge(s["product_done"], NO * g + o + 1)
                        if kind == "q":
                            if not (isinstance(g, int) and g == 0) or j >= 2:
                                act.wait_ge(s["sig_used"], 14 * g + (j - 2) + 1 if j >= 2 else 14 * g - 1)
                            nc.scalar.activation(sig[:, j % 2, 0, :], p[:, 0:GROUP], ACT.Sigmoid).then_inc(s["sig_ready"], 1)
                        elif kind == "z":
                            act.wait_ge(s["sig_used"], 14 * g + 2 + j + 1)
                            nc.scalar.activation(sig[:, j % 2, 0, :], p[:, 0:GROUP], ACT.Sigmoid, scale=-1.0)
                            nc.scalar.activation(sig[:, j % 2, 1, :], p[:, 0:GROUP], ACT.Sigmoid).then_inc(s["z_sig"], 1)
                        elif kind == "g":
                            act.wait_ge(s["sig_used"], 14 * g + 12 + j)
                            nc.scalar.activation(sigg[:], p[:], ACT.Sigmoid).then_inc(s["sigg_ready"], 1)
                        if kind == "rw" and j % 2 == 1:
                            act.wait_ge(s["product_done"], NO * g + o + 1)
                            if not (isinstance(g, int) and g == 0):
                                act.wait_ge(s["rw_stored"], 32 * g)
                            nc.scalar.activation(ro[0:width, j, :], p[0:width, 0:GROUP], ACT.Copy).then_inc(s["rw_ready"], 1)

                turn(0, 0)
                outputs(0)
                act.wait_ge(s["product_done"], NO)
                turn(1, 1)
                with act.Fori(1, NG - 1) as g:
                    outputs(g)
                    act.wait_ge(s["product_done"], NO * g + NO)
                    turn(g + 1, 1)
                outputs(NG - 1)

            @block.vector
            def _(dve):
                o_ = Order(dve, s["dve_order"])

                def norm(g):
                    dve.wait_ge(s["x_loaded"], 32 * g + 32)
                    nc.vector.bn_stats(stats[:, 0, 0, :], x[:, 0, 0:512])
                    o_.link(nc.vector.bn_stats(stats[:, 0, 1, :], x[:, 0, 512:1024]))
                    nc.vector.bn_stats(stats[:, 1, 0, :], x[:, 1, 0:512])
                    o_.count(nc.vector.bn_stats(stats[:, 1, 1, :], x[:, 1, 512:1024]))
                    o_.link(nc.vector.bn_aggr(mv[:, 0, :], stats[:, 0, :, :]))
                    nc.vector.tensor_scalar(mv[:, 0, 1:2], mv[:, 0, 1:2], LN_EPS, None, ALU.add).then_inc(s["stats_ready"], 1)
                    o_.link(nc.vector.bn_aggr(mv[:, 1, :], stats[:, 1, :, :]))
                    nc.vector.tensor_scalar(mv[:, 1, 1:2], mv[:, 1, 1:2], LN_EPS, None, ALU.add).then_inc(s["stats_ready"], 1)
                    for u in range(2):
                        dve.wait_ge(s["rstd_ready"], 2 * g + u + 1)
                        nc.vector.tensor_scalar(x[:, u, :], x[:, u, :], mv[:, u, 0:1], rstd[:, u:u + 1],
                                                ALU.subtract, ALU.mult).then_inc(s["normed"], 1)

                def turn(g, row):
                    for k in range(KD):
                        if k % 4 == 0:
                            dve.wait_ge(s["turned"], 4 * g + 2 + k // 4 + 1)
                        nc.vector.tensor_scalar(hT[:, k, P:2 * P], tp[2 + k // 4][:, (k % 4) * P:(k % 4 + 1) * P],
                                                cols[:, row, 1, k:k + 1], cols[:, row, 0, k:k + 1],
                                                ALU.mult, ALU.add).then_inc(s["hT_ready_dve"], 1)

                def outputs(g):
                    first = isinstance(g, int) and g == 0
                    for o, (kind, j, _, width) in enumerate(outs):
                        p = mp[o % 3]
                        if kind == "q":
                            dve.wait_ge(s["sig_ready"], 4 * g + j + 1)
                            if not first:
                                dve.wait_ge(s["q_stored"], 64 * g)
                            o_.link(nc.vector.tensor_tensor(qo[:, j, :], p[:, 0:GROUP], sig[:, j % 2, 0, :], ALU.mult))
                            dve.sem_inc(s["q_ready"], 1)
                            dve.sem_inc(s["sig_used"], 1)
                            dve.sem_inc(s["product_free"], 1)
                        elif kind == "z":
                            d, h = j // 4, j % 4
                            dve.wait_ge(s["z_sig"], 8 * g + j + 1)
                            if not first:
                                dve.wait_ge(s["z_stored"], 128 * g)
                            nc.vector.tensor_scalar(ko[:, d, h, :], sig[:, j % 2, 0, :], K["omlb"][:, d, h:h + 1], None, ALU.mult)
                            o_.link(nc.vector.tensor_scalar(fo[:, d, h, :], sig[:, j % 2, 1, :], K["omlb"][:, d, h:h + 1],
                                                            K["lb"][:, d, h:h + 1], ALU.mult, ALU.add))
                            dve.sem_inc(s["k_ready"], 1)
                            dve.sem_inc(s["sig_used"], 1)
                            dve.sem_inc(s["product_free"], 1)
                        elif kind == "rw" and j % 2 == 0:
                            dve.wait_ge(s["product_done"], NO * g + o + 1)
                            if not first:
                                dve.wait_ge(s["rw_stored"], 32 * g)
                            o_.link(nc.vector.tensor_copy(ro[0:width, j, :], p[0:width, 0:GROUP]))
                            dve.sem_inc(s["rw_ready"], 1)
                            dve.sem_inc(s["product_free"], 1)
                        elif kind == "rw":
                            dve.wait_ge(s["rw_ready"], 14 * g + j + 1)
                            dve.sem_inc(s["product_free"], 1)
                        elif kind == "i":
                            dve.wait_ge(s["product_done"], NO * g + o + 1)
                            if not first:
                                dve.wait_ge(s["i_stored"], 64 * g)
                            o_.link(nc.vector.tensor_copy(io[:, j, :], p[:]))
                            dve.sem_inc(s["i_ready"], 1)
                            dve.sem_inc(s["product_free"], 1)
                        else:
                            dve.wait_ge(s["sigg_ready"], 2 * g + j + 1)
                            if not first:
                                dve.wait_ge(s["g_stored"], 32 * g)
                            o_.link(nc.vector.tensor_tensor(go[:, j, :], p[:], sigg[:], ALU.mult))
                            dve.sem_inc(s["g_ready"], 1)
                            dve.sem_inc(s["sig_used"], 1)
                            dve.sem_inc(s["product_free"], 1)

                dve.wait_ge(s["cols_loaded"], 64)
                nc.vector.tensor_scalar(cols[:, :, 1, :], cols[:, :, 1, :], 1.0, None, ALU.add).then_inc(s["cols_ready"], 1)
                norm(0)
                turn(0, 0)
                n0 = o_.k

                def body(g):
                    norm(g + 1)
                    outputs(g)
                    dve.wait_ge(s["product_done"], NO * g + NO)
                    turn(g + 1, 1)
                body(0)
                o_.per = o_.k - n0
                with dve.Fori(1, NG - 1) as g:
                    o_.g, o_.k = g, n0
                    body(g)
                    assert o_.k == n0 + o_.per
                o_.g, o_.k = NG - 1, n0
                outputs(NG - 1)

            @block.tensor
            def _(pe):
                def turn(g):
                    for u in range(2):
                        pe.wait_ge(s["normed"], 2 * g + u + 1)
                        if not (isinstance(g, int) and g == 0):
                            pe.wait_ge(s["hT_ready_act"], 8 * g)
                            pe.wait_ge(s["hT_ready_dve"], 8 * g)
                        for k in range(KD):
                            t = nc.tensor.transpose(tp[2 * u + k // 4][:, (k % 4) * P:(k % 4 + 1) * P],
                                                    x[:, u, k * P:(k + 1) * P], K["ident"][:])
                            if k % 4 == 3:
                                t.then_inc(s["turned"], 1)

                def products(g, lo, hi):
                    if lo == 0:
                        pe.wait_ge(s["hT_ready_act"], 8 * g + 8)
                        pe.wait_ge(s["hT_ready_dve"], 8 * g + 8)
                    for o in range(lo, hi):
                        kind, j, c0, width = outs[o]
                        if not (isinstance(g, int) and g == 0) or o >= 3:
                            pe.wait_ge(s["product_free"], NO * g + o - 2)
                        for k in range(KD):
                            if kind in ("i", "g"):
                                mm = nc.tensor.matmul(mp[o % 3][:], hT[:, k, j * P:(j + 1) * P], w_in[:, k, c0:c0 + width],
                                                      start=(k == 0), stop=(k == KD - 1))
                            else:
                                mm = nc.tensor.matmul(mp[o % 3][0:width, 0:GROUP], w_in[:, k, c0:c0 + width], hT[:, k, :],
                                                      start=(k == 0), stop=(k == KD - 1))
                        mm.then_inc(s["product_done"], 1)

                pe.wait_ge(s["cols_ready"], 1)
                turn(0)
                pe.wait_ge(s["w_loaded"], 16 * KD)

                def body(g):
                    products(g, 0, 12)
                    turn(g + 1)
                    products(g, 12, NO)
                peel(pe, NG - 1, body)
                products(NG - 1, 0, 12)
                products(NG - 1, 12, NO)


def wait(eng, sem, value):
    if not isinstance(value, int) or value > 0:
        eng.wait_ge(sem, value)


def masks(nc, A, S, K):
    with ExitStack() as ctx:
        m = Mem(nc, ctx, "mask")
        si, ti = m.sb("s_index", [P, P], I32), m.sb("t_index", [P, P], I32)
        xi = m.sb("xor", [P, P], I32)
        sf, tf, xf = m.sb("s_float", [P, P]), m.sb("t_float", [P, P]), m.sb("xor_float", [P, P])
        ge = m.sb("xor_at_least", [P, 8, P])
        order = m.sb("s_before_t", [P, 2, P])
        bi = m.sb("block_index", [P, MAX_BLOCKS + 2], I32)
        iota_done, vo = m.sem("iota_done"), m.sem("dve_order")
        with nc.Block() as block:
            @block.gpsimd
            def _(pool):
                nc.gpsimd.iota(si[:], pattern=[[0, P]], base=0, channel_multiplier=1).then_inc(iota_done, 1)
                nc.gpsimd.iota(ti[:], pattern=[[1, P]], base=0, channel_multiplier=0).then_inc(iota_done, 1)
                nc.gpsimd.iota(bi[:], pattern=[[1, MAX_BLOCKS + 2]], base=0, channel_multiplier=0).then_inc(iota_done, 1)

            @block.vector
            def _(dve):
                o = Order(dve, vo)
                dve.wait_ge(iota_done, 3)
                nc.vector.tensor_copy(sf[:], si[:])
                nc.vector.tensor_copy(tf[:], ti[:])
                o.link(nc.vector.tensor_tensor(xi[:], si[:], ti[:], ALU.bitwise_xor))
                o.link(nc.vector.tensor_copy(xf[:], xi[:]))
                nc.vector.tensor_tensor(order[:, 0, :], tf[:], sf[:], ALU.is_gt)
                nc.vector.tensor_tensor(order[:, 1, :], sf[:], tf[:], ALU.is_gt)
                for l in range(7):
                    nc.vector.tensor_scalar(ge[:, l, :], xf[:], float(1 << l), None, ALU.is_ge)
                nc.vector.tensor_copy(K["iota"][:], bi[:])
                nc.vector.memset(K["place"][:], 0)
                nc.vector.memset(K["weight"][:], 0.0)
                nc.vector.memset(ge[:, 7, :], 0.0)
                nc.vector.memset(K["first"][:], 1.0)
                o.link(nc.vector.memset(K["one"][:], 1.0))
                nc.vector.tensor_copy(K["lt"][:], order[:, 0, :])
                for l in range(7):
                    o.link(nc.vector.tensor_tensor(xf[:], ge[:, l, :], ge[:, l + 1, :], ALU.subtract))
                    for d in range(2):
                        o.link(nc.vector.tensor_tensor(K["lvl"][:, d, l, :], xf[:], order[:, d, :], ALU.mult))
                o.link(nc.vector.tensor_scalar(xf[:], ge[:, 6, :], -1.0, 1.0, ALU.mult, ALU.add))
                for d in range(2):
                    o.link(nc.vector.tensor_tensor(K["before"][:, d, :], xf[:], order[:, d, :], ALU.mult))
                    nc.vector.tensor_tensor(K["upto"][:, d, :], K["before"][:, d, :], K["ident"][:], ALU.add)
                nc.vector.memset(K["first"][:, 0, :, 0:1], 0.0)
                nc.vector.memset(K["first"][:, 1, :, P - 1:P], 0.0)
                nc.vector.memset(K["first64"][:], 1.0)
                o.link(nc.vector.memset(K["eps"][:], 1e-19))
                nc.vector.memset(K["first64"][:, 0, :, 0:1], 0.0)
                nc.vector.memset(K["first64"][:, 1, :, RW_C - 1:RW_C], 0.0)


HG_TASKS = 16


def level_views(tile, d, level):
    half = 1 << level
    v = tile.rearrange("p h (b m) -> p (h b) m", m=2 * half)
    lo, hi = v[:, :, 0:half], v[:, :, half:2 * half]
    if d == 0:
        return v, lo, hi, v[:, :, half - 1:half]
    return v, hi, lo, v[:, :, half:half + 1]


class HgrnScan:

    def __init__(self, nc, m, S, K):
        self.nc, self.S, self.K = nc, S, K
        sb, ps, sem = m.sb, m.ps, m.sem
        self.qkf = [[sb(f"qkf{u}{d}", [P, 3, HH, P]) for d in range(2)] for u in range(2)]
        self.v = [[sb(f"v{u}{d}", [P, D_HG]) for d in range(2)] for u in range(2)]
        self.lf = [sb(f"logf{d}", [P, HH, P]) for d in range(2)]
        self.b = [sb(f"logf_sum{d}", [P, HH, P]) for d in range(2)]
        self.diff = [sb(f"exponent{r}", [P, HH, P]) for r in range(4)]
        self.z = [sb(f"scaled_qk{r}", [P, HH, P]) for r in range(4)]
        self.sc = [sb(f"scores{d}", [P, HH, P]) for d in range(2)]
        self.eb = [sb(f"decay_from_start{d}", [P, HH, P]) for d in range(2)]
        self.ekb = [sb(f"decay_to_end{d}", [P, HH, P]) for d in range(2)]
        self.khT = [sb(f"k_tokens{d}", [P, HH, P]) for d in range(2)]
        self.dl = [sb(f"decay_chunk{d}", [P, HH]) for d in range(2)]
        self.st = [sb(f"state{d}", [P, HH, P]) for d in range(2)]
        self.ob = [sb(f"o{d}", [P, HH, P]) for d in range(2)]
        self.psc = [ps(f"score_psum{r}", [P, HH, P]) for r in range(2)]
        self.pst = ps("state_psum", [P, HH, P])
        self.po = ps("out_psum", [P, HH, P])
        names = ("loaded00 loaded01 loaded10 loaded11 logf summed diff_ready exp_ready z_ready scored combined vec_ready ends_ready q_scaled k_scaled "
                 "k_turned k_copied out_done out_copied stored0 stored1 state_done state_updated order_dve state_zero inputs_used")
        self.s = {n: sem(n) for n in names.split()}

    def sync(self, sp, n, u):
        s, S = self.s, self.S
        for d in range(2):
            wait(sp, s["inputs_used"], 2 * (n - 2) + d + 1)
            sp.dma_start(self.qkf[u][d][:], S["hg_in"][d, bass.ds(n, 1)].rearrange("n x p h t -> p (n x) h t")).then_inc(s[f"loaded{u}{d}"], 16)
            sp.dma_start(self.v[u][d][:], S["hg_v"][d, bass.ds(n, 1)].rearrange("n p e -> p (n e)")).then_inc(s[f"loaded{u}{d}"], 16)

    def act(self, act, n, u):
        nc, s, K = self.nc, self.s, self.K
        for d in range(2):
            act.wait_ge(s[f"loaded{u}{d}"], 16 * (n - u) + 32)
            wait(act, s["summed"], 2 * (n - 1) + d + 1)
            nc.scalar.activation(self.lf[d][:], self.qkf[u][d][:, 2], ACT.Ln, bias=K["eps"][:, 0:1]).then_inc(s["logf"], 1)
        yield
        for d in range(2):
            end = P - 1 if d == 0 else 0
            act.wait_ge(s["summed"], 2 * n + d + 1)
            wait(act, s["q_scaled"], 2 * (n - 1) + d + 1)
            wait(act, s["k_scaled"], 2 * (n - 1) + d + 1)
            wait(act, s["state_updated"], 2 * (n - 1) + d + 1)
            nc.scalar.activation(self.eb[d][:], self.b[d][:], ACT.Exp).then_inc(s["vec_ready"], 1)
            for h in range(HH):
                nc.scalar.activation(self.ekb[d][:, h, :], self.b[d][:, h, :], ACT.Exp, scale=-1.0, bias=self.b[d][:, h, end:end + 1])
            nc.scalar.activation(self.dl[d][:], self.b[d][:, :, end:end + 1].rearrange("p h o -> p (h o)"), ACT.Exp).then_inc(s["ends_ready"], 1)
            yield
        for t in range(2, HG_TASKS):
            d, l, r = t % 2, t // 2 - 1, t % 4
            act.wait_ge(s["diff_ready"], 14 * n + t - 1)
            _, kk, qq, _ = level_views(self.diff[r][:], d, l)
            nc.scalar.activation(kk, kk, ACT.Exp, scale=-1.0)
            nc.scalar.activation(qq, qq, ACT.Exp).then_inc(s["exp_ready"], 1)
            if t in (4, 5):
                dd = t - 4
                act.wait_ge(s["k_turned"], 2 * n + dd + 1)
                nc.scalar.activation(self.khT[dd][:], self.pst[:], ACT.Copy).then_inc(s["k_copied"], 1)
            yield
        for d in range(2):
            act.wait_ge(s["out_done"], 2 * n + d + 1)
            wait(act, s[f"stored{d}"], 16 * n)
            nc.scalar.activation(self.ob[d][:], self.po[:], ACT.Copy).then_inc(s["out_copied"], 1)
            act.wait_ge(s["out_copied"], 2 * n + d + 1)
            act.dma_start(self.S["hg_o"][d, bass.ds(n, 1)].rearrange("n p (h e) -> p (n h) e", h=HH), self.ob[d][:]).then_inc(s[f"stored{d}"], 16)
            yield

    def pool(self, pool, n, u):
        nc, s = self.nc, self.s
        for d in range(2):
            pool.wait_ge(s["ends_ready"], 2 * n + d + 1)
            nc.gpsimd.tensor_tensor(self.ekb[d][:], self.qkf[u][d][:, 1], self.ekb[d][:], ALU.mult).then_inc(s["k_scaled"], 1)
            wait(pool, s["out_done"], 2 * (n - 1) + d + 1)
            nc.gpsimd.tensor_tensor(self.eb[d][:], self.qkf[u][d][:, 0], self.eb[d][:], ALU.mult).then_inc(s["q_scaled"], 1)
            yield
        for t in range(2, HG_TASKS):
            d, l, r = t % 2, t // 2 - 1, t % 4
            pool.wait_ge(s["exp_ready"], 14 * n + t - 1)
            wait(pool, s["scored"], 16 * n + t - 4 + 1)
            q, k = self.qkf[u][d][:, 0], self.qkf[u][d][:, 1]
            _, zk, zq, _ = level_views(self.z[r][:], d, l)
            _, dk, dq, _ = level_views(self.diff[r][:], d, l)
            nc.gpsimd.tensor_tensor(zk, level_views(k, d, l)[1], dk, ALU.mult)
            nc.gpsimd.tensor_tensor(zq, level_views(q, d, l)[2], dq, ALU.mult).then_inc(s["z_ready"], 1)
            yield

    def pe(self, pe, n, u):
        nc, s = self.nc, self.s
        for t in range(HG_TASKS):
            d, r = t % 2, t % 4
            wait(pe, s["combined"], 16 * n + t - 2 + 1)
            if t < 2:
                pe.wait_ge(s[f"loaded{u}{d}"], 16 * (n - u) + 32)
                for h in range(HH):
                    mm = nc.tensor.matmul(self.psc[t % 2][:, h, :], self.qkf[u][d][:, 1, h, :], self.qkf[u][d][:, 0, h, :], start=True, stop=True)
            else:
                pe.wait_ge(s["z_ready"], 14 * n + t - 1)
                for h in range(HH):
                    mm = nc.tensor.matmul(self.psc[t % 2][:, h, :], self.z[r][:, h, :], self.z[r][:, h, :], start=True, stop=True)
            mm.then_inc(s["scored"], 1)
            if t in (3, 4):
                dd = t - 3
                pe.wait_ge(s["k_scaled"], 2 * n + dd + 1)
                if dd == 0:
                    wait(pe, s["state_updated"], 2 * n)
                else:
                    pe.wait_ge(s["k_copied"], 2 * n + 1)
                for h in range(HH):
                    mm = nc.tensor.transpose(self.pst[:, h, :], self.ekb[dd][:, h, :], self.K["ident"][:])
                mm.then_inc(s["k_turned"], 1)
            yield
        for d in range(2):
            pe.wait_ge(s["q_scaled"], 2 * n + d + 1)
            pe.wait_ge(s["combined"], 16 * n + 14 + d + 1)
            if d == 0 and isinstance(n, int) and n == 0:
                pe.wait_ge(s["state_zero"], 2)
            wait(pe, s["state_updated"], 2 * (n - 1) + d + 1)
            wait(pe, s["out_copied"], 2 * n + d)
            for h in range(HH):
                nc.tensor.matmul(self.po[:, h, :], self.eb[d][:, h, :], self.st[d][:, h, :], start=True, stop=False)
                mm = nc.tensor.matmul(self.po[:, h, :], self.sc[d][:, h, :], self.v[u][d][:, h * P:(h + 1) * P], start=False, stop=True)
            mm.then_inc(s["out_done"], 1)
            pe.wait_ge(s["k_copied"], 2 * n + 2)
            wait(pe, s["state_updated"], 2 * n + d)
            for h in range(HH):
                mm = nc.tensor.matmul(self.pst[:, h, :], self.khT[d][:, h, :], self.v[u][d][:, h * P:(h + 1) * P], start=True, stop=True)
            mm.then_inc(s["state_done"], 1)
            mm = None
            yield

    def dve(self, dve, n, u):
        nc, s, K = self.nc, self.s, self.K
        flat = lambda t: t.rearrange("p h t -> p (h t)")
        for d in range(2):
            dve.wait_ge(s["logf"], 2 * n + d + 1)
            wait(dve, s["exp_ready"], 14 * n)
            rev = (lambda a: a) if d == 0 else (lambda a: a[:, ::-1])
            nc.vector.tensor_tensor_scan(rev(flat(self.b[d][:])), rev(flat(K["first"][:, d])), rev(flat(self.lf[d][:])),
                                         0.0, ALU.mult, ALU.add).then_inc(s["summed"], 1)
            yield

        def difference(t):
            d, l, r = t % 2, t // 2 - 1, t % 4
            wait(dve, s["z_ready"], 14 * n + {2: -1, 3: 0, 4: -3, 5: -2}.get(t, t - 5))
            if t < 4:
                dve.wait_ge(s["summed"], 2 * n + d + 1)
            v, _, _, _ = level_views(self.diff[r][:], d, l)
            bv, _, _, ref = level_views(self.b[d][:], d, l)
            nc.vector.tensor_tensor(v, bv, ref.broadcast_to(bv.shape), ALU.subtract).then_inc(s["diff_ready"], 1)

        for t in range(2, 5):
            difference(t)
            yield
        for t in range(HG_TASKS):
            d = t % 2
            dve.wait_ge(s["scored"], 16 * n + t + 1)
            wait(dve, s["combined"], 16 * n + t - 1)
            if t < 2:
                wait(dve, s["out_done"], 2 * (n - 1) + d + 1)
                nc.vector.tensor_tensor(self.sc[d][:], self.psc[t % 2][:], K["ident"][:].unsqueeze(1).broadcast_to([P, HH, P]),
                                        ALU.mult).then_inc(s["combined"], 1)
                if t + 5 < HG_TASKS:
                    difference(t + 5)
            else:
                if t + 5 < HG_TASKS:
                    difference(t + 5)
                else:
                    nc.vector.memset(K["spare"][:, t:t + 1], 0.0)
                nc.vector.copy_predicated(self.sc[d][:], K["lvl"][:, d, t // 2 - 1, :].bitcast(U32).unsqueeze(1).broadcast_to([P, HH, P]),
                                          self.psc[t % 2][:]).then_inc(s["combined"], 1)
            yield
        for d in range(2):
            dve.wait_ge(s["state_done"], 2 * n + d + 1)
            dve.wait_ge(s["ends_ready"], 2 * n + d + 1)
            wait(dve, s["state_updated"], 2 * (n - 1) + d + 1)
            for h in range(HH):
                i = nc.vector.scalar_tensor_tensor(self.st[d][:, h, :], self.st[d][:, h, :], self.dl[d][:, h:h + 1], self.pst[:, h, :],
                                                   ALU.mult, ALU.add)
            i.then_inc(s["state_updated"], 1)
            if d == 1:
                dve.wait_ge(s["out_done"], 2 * n + 2)
                dve.wait_ge(s["state_updated"], 2 * n + 2)
                nc.vector.memset(K["spare"][:, 0:1], 0.0).then_inc(s["inputs_used"], 2)
            yield


def run_steps(eng, steps, *programs):
    def turn(g):
        for u in range(2):
            live = [p(eng, 2 * g + u, u) for p in programs]
            while live:
                live = [x for x in live if next(x, "end") != "end"]
    peel(eng, steps // 2, turn)


def hgrn_scan(nc, A, S, K):
    with ExitStack() as ctx:
        m = Mem(nc, ctx, "hg")
        h = HgrnScan(nc, m, S, K)
        with nc.Block() as block:
            @block.sync
            def _(sp):
                peel(sp, HG_STEPS // 2, lambda g: [h.sync(sp, 2 * g + u, u) for u in range(2)])

            @block.scalar
            def _(act):
                run_steps(act, HG_STEPS, h.act)
                for d in range(2):
                    act.wait_ge(h.s[f"stored{d}"], 16 * HG_STEPS)

            @block.gpsimd
            def _(pool):
                run_steps(pool, HG_STEPS, h.pool)

            @block.vector
            def _(dve):
                for d in range(2):
                    nc.vector.memset(h.st[d][:], 0.0).then_inc(h.s["state_zero"], 1)
                dve.wait_ge(h.s["state_zero"], 2)
                run_steps(dve, HG_STEPS, h.dve)

            @block.tensor
            def _(pe):
                run_steps(pe, HG_STEPS, h.pe)


PREP_USES = ([("decay0", 0, "act"), ("decay0", 1, "act"), ("decay1", 2, "act"), ("decay1", 3, "act"),
              ("a", 0, "act"), ("a", 1, "act"), ("gate", 2, "act"), ("gate", 3, "act"),
              ("norm", 0, "dve"), ("norm", 1, "dve"), ("v", 2, "act"), ("v", 3, "act")]
             + [(f"{x}{d}", 2 * u + i, "act") for d in range(2) for u in range(2) for i, x in enumerate(("beta", "kappa"))]
             + [("bonus", 0, "dve")])
XW = NPAIR * RW_C
HEAD = 2 * XW + NPAIR
ROW = HEAD + 2 * XW


class RwkvPrep:

    def __init__(self, nc, m, A, S, K):
        self.nc, self.A, self.S, self.K = nc, A, S, K
        sb, sem = m.sb, m.sem
        self.raw = sb("raw", [P, 14, GROUP + 2 * GRID_W])
        self.mix = sb("mixed", [P, 14, GROUP])
        self.mu = sb("mu", [P, 14])
        self.col = sb("columns", [P, 6, NPAIR])
        self.w2 = sb("low_rank_w", [3 * LORA, D_RW])
        self.g2 = sb("gate_w", [GATE_LORA, D_RW])
        self.th = sb("tanh_w", [2 * LORA, GROUP])
        self.sg = sb("sig_gate", [GATE_LORA, GROUP])
        self.sw = [sb(f"decay_sig{d}", [P, NPAIR, GROUP]) for d in range(2)]
        self.a = sb("a", [P, NPAIR, GROUP])
        self.kx = sb("kk", [P, NPAIR, GROUP])
        self.t1 = sb("t1", [P, NPAIR, GROUP])
        self.pm = sb("decay", [P, NPAIR, GROUP])
        self.pi = sb("inv_decay", [P, NPAIR, GROUP])
        self.w = sb("operands", [P, 4, HEAD])
        self.bt = sb("beta", [P, NPAIR, GROUP])
        self.tm = [sb(f"tokens{u}", [P, 2, D_RW]) for u in range(2)]
        self.vt = sb("v_tokens", [P, 2, D_RW])
        self.gt = sb("gates", [P, 2, D_RW])
        self.bo = sb("bonus", [P, 2, RH])
        self.pair = sb("head_blocks", [P, P])
        self.head = sb("head_select", [P, 2])
        self.ps = [m.ps(f"bank{j}", [P, 512]) for j in range(4)]
        names = ("consts loaded blocks shifted tanh_done siglora_done filled act_emptied dve_emptied sq_ready norm_ready inv_ready "
                 "sum_ready decays_ready decays_used beta_ready w_ready w_stored tm_stored0 tm_stored1 v_stored g_stored b_stored "
                 "b_ready rb_ready order_dve order_act order_pool a_done sync_turns").split()
        self.s = {n: sem(n) for n in names}
        self.o = {}

    def consts(self, sp):
        A, s = self.A, self.s
        sp.dma_start(self.mu[:, 0:12], A["rw_mu"][0, 0:12 * P].rearrange("(t p) -> p t", p=P)).then_inc(s["consts"], 16)
        sp.dma_start(self.mu[0:GATE_LORA, 12:14], A["rw_mu"][0, 12 * P:].rearrange("(t p) -> p t", p=GATE_LORA)).then_inc(s["consts"], 16)
        for j, src in enumerate((A["rw_w0"][0, 0], A["rw_w0"][0, 1], A["rw_a0"][0], A["rw_k_k"][0], A["rw_k_a"][0],
                                 A["rw_r_k"][0].rearrange("h j -> (h j)"))):
            sp.dma_start(self.col[:, j, :], src.rearrange("(t p) -> p t", p=P)).then_inc(s["consts"], 16)
        for d in range(2):
            sp.dma_start(self.w2[d * LORA:(d + 1) * LORA, :], A["rw_w_decay2"][0, d]).then_inc(s["consts"], 16)
        sp.dma_start(self.w2[2 * LORA:, :], A["rw_w_a2"][0]).then_inc(s["consts"], 16)
        sp.dma_start(self.g2[:], A["rw_w_g2"][0]).then_inc(s["consts"], 16)

    N_CONSTS = 16 * 12

    def steps_of(self, g, ctx_group, c):
        if ctx_group:
            return c, 3 - c
        return 4 * g + c, (RW_STEPS + 3 - c) - 4 * g

    def load(self, sp, g, ctx_group):
        s = self.s
        if ctx_group:
            sp.dma_start(self.raw[:, 0:12, 0:CTX + 2], self.S["rw_ctx"][0:12].rearrange("t p c -> p t c")).then_inc(s["loaded"], 16)
            sp.dma_start(self.raw[0:GATE_LORA, 12:14, 0:CTX + 2], self.S["rw_ctx"][12:14, 0:GATE_LORA].rearrange("t p c -> p t c")).then_inc(s["loaded"], 16)
        else:
            sp.wait_ge(s["shifted"], g)
            w = GROUP + 2 * GRID_W
            sp.dma_start(self.raw[:, 0:12, :], self.S["rw_lat"][0:12, :, bass.ds(g * GROUP - GROUP, w)].rearrange("t p c -> p t c")).then_inc(s["loaded"], 16)
            sp.dma_start(self.raw[0:GATE_LORA, 12:14, :], self.S["rw_lat"][12:14, 0:GATE_LORA, bass.ds(g * GROUP - GROUP, w)].rearrange("t p c -> p t c")).then_inc(s["loaded"], 16)

    def store(self, sp, g, ctx_group):
        S, s = self.S, self.s
        sp.wait_ge(s["act_emptied"], 18 * g + 8)
        sp.sem_inc(s["sync_turns"], 1)
        row = g * GROUP
        for u in range(2):
            sp.dma_start(S["rw_g"][bass.ds(row + u * P, P), :], self.gt[:, u, :]).then_inc(s["g_stored"], 16)
        sp.wait_ge(s["act_emptied"], 18 * g + 10)
        sp.sem_inc(s["sync_turns"], 1)
        for u in range(2):
            for c in range(2):
                for n, d in zip(self.steps_of(g, ctx_group, 2 * u + c), range(2)):
                    sp.dma_start(S["rw_tm"][d, bass.ds(n, 1), :, 2, :].rearrange("n s e -> s (n e)"),
                                 self.vt[c * RW_C:(c + 1) * RW_C, u, :]).then_inc(s["v_stored"], 16)
        for d in range(2):
            sp.wait_ge(s["w_ready"], 2 * g + d + 1)
            sp.sem_inc(s["sync_turns"], 1)
            for c in range(4):
                n = self.steps_of(g, ctx_group, c)[d]
                row_n = S["rw_in"][d, bass.ds(n, 1)].rearrange("n p x -> p (n x)")
                sp.dma_start(row_n[:, 0:HEAD], self.w[:, c, :]).then_inc(s["w_stored"], 16)
                for x, src in enumerate((self.bt, self.pi)):
                    sp.dma_start(row_n[:, HEAD + x * XW:HEAD + (x + 1) * XW].rearrange("p (j t) -> p j t", t=RW_C),
                                 src[:, :, c * RW_C:(c + 1) * RW_C]).then_inc(s["w_stored"], 16)
            for u in range(2):
                sp.wait_ge(s["act_emptied"], 18 * g + 10 + 4 * d + 2 * u + 2)
                sp.sem_inc(s["sync_turns"], 1)
                for c in range(2):
                    n = self.steps_of(g, ctx_group, 2 * u + c)[d]
                    sp.dma_start(S["rw_tm"][d, bass.ds(n, 1), :, 0:2, :].rearrange("n s x e -> s (n x) e"),
                                 self.tm[u][c * RW_C:(c + 1) * RW_C]).then_inc(s[f"tm_stored{u}"], 16)
        sp.wait_ge(s["b_ready"], g + 1)
        sp.sem_inc(s["sync_turns"], 1)
        for u in range(2):
            sp.dma_start(S["rw_bonus"][bass.ds(row + u * P, P), :], self.bo[:, u, :]).then_inc(s["b_stored"], 16)

    def finish(self, sp):
        for n, per in (("g_stored", 2), ("v_stored", 8), ("w_stored", 24), ("tm_stored0", 4), ("tm_stored1", 4), ("b_stored", 2)):
            sp.wait_ge(self.s[n], 16 * per * NG)

    def pool_start(self, pool):
        nc, s = self.nc, self.s
        o = Order(pool, s["order_pool"])
        o.link(nc.gpsimd.memset(self.raw[GATE_LORA:, 12:14, :], 0.0))
        o.link(nc.gpsimd.memset(self.mu[GATE_LORA:, 12:14], 0.0))
        o.link(nc.gpsimd.memset(self.pair[:], 0.0))
        o.link(nc.gpsimd.memset(self.head[:], 0.0))
        for h in range(2):
            o.link(nc.gpsimd.memset(self.pair[h * 64:(h + 1) * 64, h * 64:(h + 1) * 64], 1.0))
            o.link(nc.gpsimd.memset(self.head[h * 64:(h + 1) * 64, h:h + 1], 1.0))
        pool.sem_inc(s["blocks"], 1)

    def act(self, act, g, ctx_group):
        nc, s = self.nc, self.s
        act.wait_ge(s["shifted"], g + 1)
        wait(act, s["filled"], 21 * (g - 1) + 8)
        nc.scalar.activation(self.th[:], self.mix[0:2 * LORA, 12, :], ACT.Tanh).then_inc(s["tanh_done"], 1)
        nc.scalar.activation(self.sg[:], self.mix[0:GATE_LORA, 13, :], ACT.Sigmoid).then_inc(s["siglora_done"], 1)
        yield
        for i in range(6):
            dst = (self.sw[0], self.sw[1], self.a)[i // 2]
            if i == 0:
                wait(act, s["sum_ready"], 2 * g)
                wait(act, s["a_done"], g)
            act.wait_ge(s["filled"], 21 * g + i + 1)
            for j in range(2):
                t = 2 * (i % 2) + j
                ins = nc.scalar.activation(dst[:, t, :], self.ps[PREP_USES[i][1]][:, j * GROUP:(j + 1) * GROUP], ACT.Sigmoid,
                                           bias=self.col[:, i // 2, t:t + 1])
            ins.then_inc(s["act_emptied"], 1)
            yield
        for u in range(2):
            act.wait_ge(s["filled"], 21 * g + 7 + u)
            if u == 0:
                wait(act, s["g_stored"], 32 * g)
            nc.scalar.activation(self.gt[:, u, :], self.ps[2 + u][:], ACT.Copy).then_inc(s["act_emptied"], 1)
        act.wait_ge(s["norm_ready"], g + 1)
        nc.scalar.activation(self.t1[:], self.t1[:], ACT.Ln).then_inc(s["order_act"], 1)
        act.wait_ge(s["order_act"], g + 1)
        nc.scalar.activation(self.t1[:], self.t1[:], ACT.Exp, scale=-0.5).then_inc(s["inv_ready"], 1)
        yield
        for u in range(2):
            act.wait_ge(s["filled"], 21 * g + 11 + u)
            if u == 0:
                wait(act, s["v_stored"], 128 * g)
            nc.scalar.activation(self.vt[:, u, :], self.ps[2 + u][:], ACT.Copy).then_inc(s["act_emptied"], 1)
        yield
        for d in range(2):
            act.wait_ge(s["sum_ready"], 2 * g + d + 1)
            wait(act, s["w_ready"], 2 * g + d)
            wait(act, s["w_stored"], 16 * (24 * g + 12 * d))
            wait(act, s["filled"], 21 * g + 16 if d else 21 * (g - 1) + 20)
            nc.scalar.activation(self.pm[:], self.sw[d][:], ACT.Exp, scale=-DECAY)
            nc.scalar.activation(self.pi[:], self.sw[d][:], ACT.Exp, scale=DECAY).then_inc(s["decays_ready"], 1)
            yield
            for u in range(2):
                for i in range(2):
                    use = 12 + 4 * d + 2 * u + i
                    act.wait_ge(s["filled"], 21 * g + use + 1)
                    if i == 0:
                        wait(act, s[f"tm_stored{u}"], 16 * (4 * g + 2 * d))
                    nc.scalar.activation(self.tm[u][:, i, :], self.ps[PREP_USES[use][1]][:], ACT.Copy).then_inc(s["act_emptied"], 1)
            yield

    def pe(self, pe, g, ctx_group):
        nc, s, mix = self.nc, self.s, self.mix

        def emptied(i):
            bank = PREP_USES[i][1]
            before = [j for j in range(i) if PREP_USES[j][1] == bank]
            gg, j = (g, before[-1]) if before else (g - 1, max(j for j in range(21) if PREP_USES[j][1] == bank))
            eng = PREP_USES[j][2]
            per = {"act": 18, "dve": 3}[eng]
            count = sum(1 for x in PREP_USES[:j + 1] if x[2] == eng)
            wait(pe, s[eng + "_emptied"], per * gg + count)

        ps = self.ps
        pe.wait_ge(s["tanh_done"], g + 1)
        if isinstance(g, int) and g == 0:
            pe.wait_ge(s["blocks"], 1)
            pe.wait_ge(s["consts"], self.N_CONSTS)
        for i in range(6):
            emptied(i)
            r = i // 2
            src = self.th[r * LORA:(r + 1) * LORA, :] if r < 2 else mix[2 * LORA:3 * LORA, 12, :]
            for j in range(2):
                t = 2 * (i % 2) + j
                mm = nc.tensor.matmul(ps[PREP_USES[i][1]][:, j * GROUP:(j + 1) * GROUP], self.w2[r * LORA:(r + 1) * LORA, t * P:(t + 1) * P],
                                      src, start=True, stop=True)
            mm.then_inc(s["filled"], 1)
        yield
        pe.wait_ge(s["siglora_done"], g + 1)
        for u in range(2):
            emptied(6 + u)
            nc.tensor.matmul(ps[2 + u][:], self.sg[:, u * P:(u + 1) * P], self.g2[:], start=True, stop=True).then_inc(s["filled"], 1)
        yield
        pe.wait_ge(s["sq_ready"], g + 1)
        for i in range(2):
            emptied(8 + i)
            nc.tensor.matmul(ps[i][:], self.pair[:], self.t1[:, 2 * i:2 * i + 2, :].rearrange("p t c -> p (t c)"),
                             start=True, stop=True).then_inc(s["filled"], 1)
        yield
        for u in range(2):
            emptied(10 + u)
            for t in range(4):
                mm = nc.tensor.transpose(ps[2 + u][:, t * P:(t + 1) * P], mix[:, 8 + t, u * P:(u + 1) * P], self.K["ident"][:])
            mm.then_inc(s["filled"], 1)
        yield
        for d in range(2):
            pe.wait_ge(s["w_ready"], 2 * g + d + 1)
            for u in range(2):
                for i in range(2):
                    use = 12 + 4 * d + 2 * u + i
                    emptied(use)
                    for t in range(4):
                        mm = nc.tensor.transpose(ps[PREP_USES[use][1]][:, t * P:(t + 1) * P], (self.bt, self.pi)[i][:, t, u * P:(u + 1) * P], self.K["ident"][:])
                    mm.then_inc(s["filled"], 1)
            yield
        pe.wait_ge(s["rb_ready"], g + 1)
        emptied(20)
        for u in range(2):
            for t in range(4):
                mm = nc.tensor.matmul(ps[0][:, u * RH + 2 * t:u * RH + 2 * t + 2], self.t1[:, t, u * P:(u + 1) * P], self.head[:],
                                      start=True, stop=True)
        mm.then_inc(s["filled"], 1)
        yield

    def dve(self, dve, g, ctx_group, o):
        nc, s, raw, mix, V = self.nc, self.s, self.raw, self.mix, self.nc.vector
        dve.wait_ge(s["loaded"], 32 * g + 32)
        wait(dve, s["filled"], 21 * g)
        if ctx_group:
            dve.wait_ge(s["consts"], self.N_CONSTS)
            dve.wait_ge(s["blocks"], 1)
            o.link(V.tensor_tensor(mix[:], raw[:, :, 0:GROUP], raw[:, :, 2:GROUP + 2], ALU.add))
            own, scale = raw[:, :, 1:GROUP + 1], 0.5
            o.count(V.memset(self.K["spare"][:, 16:17], 0.0))
            o.count(V.memset(self.K["spare"][:, 17:18], 0.0))
        else:
            own, scale = raw[:, :, GRID_W:GRID_W + GROUP], 0.25
            grid = lambda t, a, b: t.rearrange("p t (r c) -> p t r c", c=GRID_W)[:, :, :, a:b]
            o.link(V.tensor_tensor(mix[:], raw[:, :, 0:GROUP], raw[:, :, 2 * GRID_W:], ALU.add))
            yield
            o.link(V.tensor_tensor(grid(mix[:], 1, GRID_W), grid(mix[:], 1, GRID_W), grid(own, 0, GRID_W - 1), ALU.add))
            yield
            o.link(V.tensor_tensor(grid(mix[:], 0, GRID_W - 1), grid(mix[:], 0, GRID_W - 1), grid(own, 1, GRID_W), ALU.add))
        yield
        o.link(V.scalar_tensor_tensor(mix[:], mix[:], scale, own, ALU.mult, ALU.subtract))
        yield
        o.link(V.tensor_tensor(mix[:], mix[:], self.mu[:].unsqueeze(2).broadcast_to([P, 14, GROUP]), ALU.mult))
        yield
        o.link(V.tensor_tensor(mix[:], mix[:], own, ALU.add))
        dve.sem_inc(s["shifted"], 1)
        yield
        col = lambda j: self.col[:, j, :].unsqueeze(2).broadcast_to([P, NPAIR, GROUP])
        r, k, v = mix[:, 0:4], mix[:, 4:8], mix[:, 8:12]
        kx, t1, a, w = self.kx, self.t1, self.a, self.w
        o.link(V.tensor_tensor(kx[:], k, col(3), ALU.mult))
        o.link(V.tensor_tensor(t1[:], kx[:], kx[:], ALU.mult))
        dve.sem_inc(s["sq_ready"], 1)
        yield
        dve.wait_ge(s["act_emptied"], 18 * g + 6)
        o.link(V.tensor_scalar(self.pm[:], a[:], 1.0, None, ALU.subtract))
        o.link(V.tensor_tensor(self.pm[:], self.pm[:], col(4), ALU.mult))
        yield
        o.link(V.scalar_tensor_tensor(k, self.pm[:], 1.0, k, ALU.add, ALU.mult))
        yield
        for i in range(2):
            dve.wait_ge(s["filled"], 21 * g + 9 + i)
            if i == 0:
                dve.wait_ge(s["filled"], 21 * g + 10)
            o.link(V.tensor_scalar(t1[:, 2 * i:2 * i + 2, :].rearrange("p t c -> p (t c)"), self.ps[i][:], 1e-12, None, ALU.max))
            dve.sem_inc(s["dve_emptied"], 1)
        dve.sem_inc(s["norm_ready"], 1)
        yield
        chunks = lambda t: t.rearrange("p j (c t) -> p (j c) t", t=RW_C)
        flat = lambda t: t.rearrange("p x t -> p (x t)")
        for d in range(2):
            rev = (lambda x: x) if d == 0 else (lambda x: x[:, ::-1])
            sw = rev(flat(self.sw[d][:]))
            o.link(V.tensor_tensor_scan(sw, rev(flat(self.K["first64"][:, d])), sw, 0.0, ALU.mult, ALU.add))
            dve.sem_inc(s["sum_ready"], 1)
            yield
        dve.wait_ge(s["inv_ready"], g + 1)
        o.link(V.tensor_tensor(kx[:], kx[:], t1[:], ALU.mult))
        yield
        o.link(V.scalar_tensor_tensor(a[:], kx[:], -1.0, a[:], ALU.mult, ALU.mult))
        yield
        by_chunk = lambda t: t.rearrange("p j (c t) -> p c j t", t=RW_C)
        out = lambda x: w[:, :, x * XW:(x + 1) * XW].rearrange("p c (j t) -> p c j t", t=RW_C)
        for d in range(2):
            dve.wait_ge(s["decays_ready"], 2 * g + d + 1)
            wait(dve, s["w_stored"], 16 * (24 * g + 12 * d))
            if d == 1:
                dve.wait_ge(s["filled"], 21 * g + 16)
            pm, pi = self.pm, self.pi
            kv, pv, ov = by_chunk(kx[:]), by_chunk(pm[:]), out(0)
            first, rest, before, end = (0, slice(1, RW_C), slice(0, RW_C - 1), RW_C - 1) if d == 0 else (RW_C - 1, slice(0, RW_C - 1), slice(1, RW_C), 0)
            for c in range(4):
                V.tensor_tensor(ov[:, c, :, rest], kv[:, c, :, rest], pv[:, c, :, before], ALU.mult)
            V.tensor_copy(ov[:, :, :, first], kv[:, :, :, first])
            V.tensor_copy(w[:, :, 2 * XW:], pv[:, :, :, end])
            yield
            V.tensor_tensor(out(1), by_chunk(r), pv, ALU.mult)
            yield
            V.tensor_tensor(self.bt[:], a[:], pi[:], ALU.mult)
            yield
            o.link(V.tensor_tensor(pi[:], k, pi[:], ALU.mult))
            dve.sem_inc(s["w_ready"], 1)
            if d == 1:
                dve.sem_inc(s["a_done"], 1)
            yield
        o.link(V.tensor_tensor(t1[:], r, k, ALU.mult))
        o.link(V.tensor_tensor(t1[:], t1[:], col(5), ALU.mult))
        dve.sem_inc(s["rb_ready"], 1)
        yield
        dve.wait_ge(s["filled"], 21 * g + 21)
        wait(dve, s["b_stored"], 32 * g)
        o.link(V.tensor_copy(self.bo[:].rearrange("p u h -> p (u h)"), self.ps[0][:, 0:2 * RH]))
        dve.sem_inc(s["dve_emptied"], 1)
        dve.sem_inc(s["b_ready"], 1)
        yield


def drain(gen):
    for _ in gen:
        pass


def groups(eng, body):
    body(0, True)
    with eng.Fori(1, NG) as g:
        body(g, False)


def rwkv_prep(nc, A, S, K):
    with ExitStack() as ctx:
        m = Mem(nc, ctx, "prep")
        p = RwkvPrep(nc, m, A, S, K)
        with nc.Block() as block:
            @block.sync
            def _(sp):
                p.consts(sp)
                groups(sp, lambda g, c: (p.load(sp, g, c), p.store(sp, g, c)))
                p.finish(sp)

            @block.gpsimd
            def _(pool):
                p.pool_start(pool)

            @block.scalar
            def _(act):
                groups(act, lambda g, c: drain(p.act(act, g, c)))

            @block.tensor
            def _(pe):
                groups(pe, lambda g, c: drain(p.pe(pe, g, c)))

            @block.vector
            def _(dve):
                o = Order(dve, p.s["order_dve"])

                def body(g, c):
                    o.g, o.k = g, 0
                    drain(p.dve(dve, g, c, o))
                    if c:
                        o.per = o.k
                    assert o.k == o.per
                groups(dve, body)


class RwkvScan:

    def __init__(self, nc, m, S, K):
        self.nc, self.S, self.K = nc, S, K
        sb, sem = m.sb, m.sem
        two = lambda f: [[f(u, d) for d in range(2)] for u in range(2)]
        self.head = two(lambda u, d: sb(f"alpha_rho{u}{d}", [P, HEAD]))
        self.bd = two(lambda u, d: sb(f"blocks{u}{d}", [P, 4, NPAIR, P]))
        self.tm = two(lambda u, d: sb(f"tokens{u}{d}", [P, 2, NPAIR, P]))
        self.v = two(lambda u, d: sb(f"v{u}{d}", [P, NPAIR, RW_C]))
        self.rb = two(lambda u, d: sb(f"rho_beta{u}{d}", [P, NPAIR, P]))
        self.kk = two(lambda u, d: sb(f"kappas{u}{d}", [P, 2, NPAIR, P]))
        self.r = two(lambda u, d: sb(f"inverse{u}{d}", [P, NPAIR, P]))
        one = lambda name, shape: [sb(f"{name}{d}", shape) for d in range(2)]
        self.at, self.t, self.x = one("A", [P, NPAIR, P]), one("T", [P, NPAIR, P]), one("X", [P, NPAIR, P])
        self.al = [[sb(f"A_level{d}{i}", [P, NPAIR, P]) for i in range(2)] for d in range(2)]
        self.st, self.rhs, self.uu, self.y = (one(x, [P, NPAIR, RW_C]) for x in ("state", "rhs", "u", "y"))
        self.pa = [m.ps(f"inverse_bank{d}", [P, NPAIR, P]) for d in range(2)]
        self.pb = [m.ps(f"chain_bank{d}", [P, 2, NPAIR, RW_C]) for d in range(2)]
        names = ("grams masked level_ready r_ready t_psum t_ready x_psum x_ready rd_psum "
                 "rhs_psum rhs_ready u_psum u_ready y_psum y_ready s_psum s_ready s_order y_stored").split()
        self.s = [{n: sem(f"{n}{d}") for n in names} for d in range(2)]
        self.loaded = two(lambda u, d: sem(f"loaded{u}{d}"))
        self.zeroed, self.zeroed_pool = sem("zeroed"), sem("zeroed_pool")

    N_LOADS = 9

    def sync(self, sp, n, u):
        S = self.S
        for d in range(2):
            s, got = self.s[d], self.loaded[u][d]
            wait(sp, s["s_ready"], n - 1)
            row = S["rw_in"][d, bass.ds(n, 1)].rearrange("n p x -> p (n x)")
            tok = S["rw_tm"][d, bass.ds(n, 1)].rearrange("n s x (j h e) -> h s (n x) j e", h=2, e=RW_C)
            sp.dma_start(self.head[u][d][:], row[:, 0:HEAD]).then_inc(got, 16)
            for h in range(2):
                q = slice(h * RW_C, (h + 1) * RW_C)
                for x0, c0 in ((0, 0), (2, HEAD)):
                    sp.dma_start(self.bd[u][d][q, x0:x0 + 2, :, q], row[q, c0:c0 + 2 * XW].rearrange("p (x j t) -> p x j t", x=2, j=NPAIR)).then_inc(got, 16)
                sp.dma_start(self.tm[u][d][q, :, :, q], tok[h, :, 0:2]).then_inc(got, 16)
                sp.dma_start(self.v[u][d][q], tok[h, :, 2]).then_inc(got, 16)

    def zero_dve(self, dve):
        V = self.nc.vector
        for d in range(2):
            V.memset(self.st[d][:], 0.0)
            V.memset(self.at[d][:], 0.0)
            for u in range(2):
                V.memset(self.rb[u][d][:], 0.0)
                V.memset(self.kk[u][d][:], 0.0)
        V.memset(self.K["spare"][:, 20:21], 0.0).then_inc(self.zeroed, 1)
        dve.wait_ge(self.zeroed, 1)

    def zero_pool(self, pool):
        for u in range(2):
            for d in range(2):
                i = self.nc.gpsimd.memset(self.bd[u][d][:], 0.0)
                i = self.nc.gpsimd.memset(self.tm[u][d][:], 0.0)
        i.then_inc(self.zeroed_pool, 1)

    def got(self, n, u):
        return 8 * self.N_LOADS * (n - u) + 16 * self.N_LOADS

    def pe(self, pe, n, u, chain_only=False):
        nc, w = self.nc, 1 - u

        def rhs(d):
            s = self.s[d]
            wait(pe, s["s_ready"], n - 1)
            wait(pe, s["y_ready"], n - 1)
            pe.wait_ge(s["masked"], 2 * n)
            for j in range(NPAIR):
                nc.tensor.matmul(self.pb[d][:, 0, j, :], self.bd[w][d][:, 0, j, :], self.st[d][:, j, :], start=True, stop=False)
                i = nc.tensor.matmul(self.pb[d][:, 0, j, :], self.kk[w][d][:, 0, j, :], self.v[w][d][:, j, :], start=False, stop=True)
            i.then_inc(s["rhs_psum"], 1)

        def solve(d):
            s = self.s[d]
            pe.wait_ge(s["rhs_ready"], n)
            pe.wait_ge(s["r_ready"], 6 * n)
            for j in range(NPAIR):
                i = nc.tensor.matmul(self.pb[d][:, 1, j, :], self.r[w][d][:, j, :], self.rhs[d][:, j, :], start=True, stop=True)
            i.then_inc(s["u_psum"], 1)

        def out(d):
            s = self.s[d]
            pe.wait_ge(s["u_ready"], n)
            for j in range(NPAIR):
                o = self.pb[d][:, 0, j, :]
                nc.tensor.matmul(o, self.bd[w][d][:, 1, j, :], self.st[d][:, j, :], start=True, stop=False)
                nc.tensor.matmul(o, self.kk[w][d][:, 1, j, :], self.v[w][d][:, j, :], start=False, stop=False)
                i = nc.tensor.matmul(o, self.rb[w][d][:, j, :], self.uu[d][:, j, :], start=False, stop=True)
            i.then_inc(s["y_psum"], 1)

        def state(d):
            s = self.s[d]
            pe.wait_ge(s["y_ready"], n)
            for j in range(NPAIR):
                o = self.pb[d][:, 1, j, :]
                nc.tensor.matmul(o, self.tm[w][d][:, 1, j, :], self.v[w][d][:, j, :], start=True, stop=False)
                i = nc.tensor.matmul(o, self.tm[w][d][:, 0, j, :], self.uu[d][:, j, :], start=False, stop=True)
            i.then_inc(s["s_psum"], 1)

        def gram(d, k):
            s = self.s[d]
            if k == 0:
                pe.wait_ge(self.loaded[u][d], self.got(n, u))
                wait(pe, s["r_ready"], 6 * n)
            else:
                pe.wait_ge(s["masked"], 2 * n + 1)
            for j in range(NPAIR):
                both = self.head[u][d][:, 0:2 * XW].rearrange("p (x j t) -> p x j t", x=2, j=NPAIR)[:, :, j, :]
                i = nc.tensor.matmul(self.pa[d][:, j, :], self.bd[u][d][:, 2 + k, j, :], both, start=True, stop=True)
            i.then_inc(s["grams"], 1)

        def turn(d, l):
            s = self.s[d]
            pe.wait_ge(s["r_ready"], 6 * n + l)
            if l == 1:
                pe.wait_ge(s["masked"], 2 * n + 2)
            for j in range(NPAIR):
                i = nc.tensor.transpose(self.pa[d][:, j, :], self.r[u][d][:, j, :], self.K["ident"][:])
            i.then_inc(s["t_psum"], 1)

        def cross(d, l):
            s = self.s[d]
            pe.wait_ge(s["t_ready"], 5 * n + l)
            pe.wait_ge(s["level_ready"], 6 * n + l + 1)
            for j in range(NPAIR):
                i = nc.tensor.matmul(self.pa[d][:, j, :], self.al[d][l % 2][:, j, :], self.t[d][:, j, :], start=True, stop=True)
            i.then_inc(s["x_psum"], 1)

        def grow(d, l):
            s = self.s[d]
            pe.wait_ge(s["x_ready"], 5 * n + l)
            for j in range(NPAIR):
                i = nc.tensor.matmul(self.pa[d][:, j, :], self.x[d][:, j, :], self.r[u][d][:, j, :], start=True, stop=True)
            i.then_inc(s["rd_psum"], 1)

        chain = [] if isinstance(n, int) and n == 0 else [rhs, solve, out, state]
        if chain_only:
            for f in chain:
                f(0)
                f(1)
            return
        if isinstance(n, int) and n == 0:
            pe.wait_ge(self.zeroed, 1)
        work = [lambda d: gram(d, 0), lambda d: gram(d, 1), lambda d: turn(d, 1)]
        for l in range(1, 6):
            work += [lambda d, l=l: cross(d, l), lambda d, l=l: grow(d, l)]
            if l < 5:
                work += [lambda d, l=l: turn(d, l + 1)]
        for i, f in enumerate(work):
            for d in range(2):
                f(d)
                yield
            if i % 2 == 0 and chain:
                c = chain.pop(0)
                for d in range(2):
                    c(d)
                    yield

    def act(self, act, n, u, chain_only=False):
        nc = self.nc

        def rhs(d):
            s = self.s[d]
            act.wait_ge(s["rhs_psum"], n)
            nc.scalar.activation(self.rhs[d][:], self.pb[d][:, 0], ACT.Copy).then_inc(s["rhs_ready"], 1)

        def solve(d):
            s = self.s[d]
            act.wait_ge(s["u_psum"], n)
            wait(act, s["s_psum"], n - 1)
            nc.scalar.activation(self.uu[d][:], self.pb[d][:, 1], ACT.Copy).then_inc(s["u_ready"], 1)

        def out(d):
            s = self.s[d]
            act.wait_ge(s["y_psum"], n)
            wait(act, s["y_stored"], 16 * (n - 1))
            nc.scalar.activation(self.y[d][:], self.pb[d][:, 0], ACT.Copy).then_inc(s["y_ready"], 1)

        def copies(d, l, name):
            s = self.s[d]
            dst = self.t if name == "t" else self.x
            act.wait_ge(s[f"{name}_psum"], 5 * n + l)
            nc.scalar.activation(dst[d][:], self.pa[d][:], ACT.Copy).then_inc(s[f"{name}_ready"], 1)

        chain = [] if isinstance(n, int) and n == 0 else [rhs, solve, out]
        if chain_only:
            for f in chain:
                f(0)
                f(1)
            return
        work = [None, None, (1, "t")]
        for l in range(1, 6):
            work += [(l, "x"), None]
            if l < 5:
                work += [(l + 1, "t")]
        for i, f in enumerate(work):
            for d in range(2):
                if f:
                    copies(d, *f)
                yield
            if i % 2 == 0 and chain:
                c = chain.pop(0)
                for d in range(2):
                    c(d)
                    yield

    def store(self, eng, n):
        for d in range(2):
            s = self.s[d]
            eng.wait_ge(s["y_ready"], n)
            eng.dma_start(self.S["rw_y"][d, bass.ds(n - 1, 1)].rearrange("n p j e -> p (n j) e"), self.y[d][:]).then_inc(s["y_stored"], 16)

    def pool(self, pool, n, u):
        nc = self.nc
        for l in range(6):
            for d in range(2):
                s = self.s[d]
                if l == 0:
                    pool.wait_ge(s["masked"], 2 * n + 1)
                if l == 2:
                    pool.wait_ge(s["r_ready"], 6 * n + 1)
                else:
                    wait(pool, s["x_psum"], 5 * n + {0: -1, 1: 0, 3: 1, 4: 2, 5: 3}[l])
                nc.gpsimd.tensor_tensor(self.al[d][l % 2][:], self.at[d][:], self.K["lvl"][:, d, l, :].unsqueeze(1).broadcast_to([P, NPAIR, P]),
                                        ALU.mult).then_inc(s["level_ready"], 1)
                yield

    def dve(self, dve, n, u, chain_only=False):
        nc, K, V, w = self.nc, self.K, self.nc.vector, 1 - u
        halves = [slice(h * RW_C, (h + 1) * RW_C) for h in range(2)]

        def mask(d, k):
            s = self.s[d]
            dve.wait_ge(s["grams"], 2 * n + k + 1)
            if k == 0:
                wait(dve, s["level_ready"], 6 * n)
            wait(dve, s["y_psum"], n - 1)
            for q in halves:
                for x, name in enumerate(("before", "upto")):
                    dst = ((self.at[d], self.rb[u][d]) if k == 0 else (self.kk[u][d][:, 0], self.kk[u][d][:, 1]))[x]
                    i = V.tensor_tensor(dst[q, :, q], self.pa[d][q, :, x * RW_C:(x + 1) * RW_C],
                                        K[name][q, d, q].unsqueeze(1).broadcast_to([RW_C, NPAIR, RW_C]), ALU.mult)
            i.then_inc(s["masked"], 1)

        def inverse(d, l):
            s = self.s[d]
            if l == 0:
                dve.wait_ge(s["level_ready"], 6 * n + 1)
                wait(dve, s["u_psum"], n - 1)
                V.tensor_tensor(self.r[u][d][:], self.al[d][0][:], K["ident"][:].unsqueeze(1).broadcast_to([P, NPAIR, P]), ALU.add)\
                    .then_inc(s["r_ready"], 1)
            else:
                dve.wait_ge(s["rd_psum"], 5 * n + l)
                dve.wait_ge(s["r_ready"], 6 * n + l)
                V.tensor_tensor(self.r[u][d][:], self.r[u][d][:], self.pa[d][:], ALU.add).then_inc(s["r_ready"], 1)

        def state(d):
            s = self.s[d]
            dve.wait_ge(s["s_psum"], n)
            wait(dve, s["s_ready"], n - 1)
            V.tensor_tensor(self.st[d][:], self.st[d][:], self.pb[d][:, 1], ALU.add).then_inc(s["s_order"], 1)
            dve.wait_ge(s["s_order"], n)
            V.tensor_tensor(self.st[d][:], self.st[d][:], self.head[w][d][:, 2 * XW:HEAD].unsqueeze(2).broadcast_to([P, NPAIR, RW_C]),
                            ALU.mult).then_inc(s["s_ready"], 1)

        if chain_only:
            state(0)
            state(1)
            return
        work = [lambda d: mask(d, 0), lambda d: mask(d, 1), lambda d: inverse(d, 0)] + [lambda d, l=l: inverse(d, l) for l in range(1, 6)]
        for i, f in enumerate(work):
            for d in range(2):
                f(d)
                yield
            if i == 4 and not (isinstance(n, int) and n == 0):
                for d in range(2):
                    state(d)
                    yield


def rwkv_scan(nc, A, S, K):
    with ExitStack() as ctx:
        m = Mem(nc, ctx, "rw")
        r = RwkvScan(nc, m, S, K)
        with nc.Block() as block:
            @block.sync
            def _(sp):
                sp.wait_ge(r.zeroed_pool, 1)

                def turn(g):
                    for u in range(2):
                        r.sync(sp, 2 * g + u, u)
                peel(sp, RW_STEPS // 2, turn)

            @block.gpsimd
            def _(pool):
                r.zero_pool(pool)

                def turn(g):
                    for u in range(2):
                        drain(r.pool(pool, 2 * g + u, u))
                        if not (isinstance(g, int) and g == 0 and u == 0):
                            r.store(pool, 2 * g + u)
                peel(pool, RW_STEPS // 2, turn)
                r.store(pool, RW_STEPS)
                for d in range(2):
                    pool.wait_ge(r.s[d]["y_stored"], 16 * RW_STEPS)

            @block.scalar
            def _(act):
                run_steps(act, RW_STEPS, r.act)
                drain(r.act(act, RW_STEPS, 0, True))

            @block.tensor
            def _(pe):
                run_steps(pe, RW_STEPS, r.pe)
                drain(r.pe(pe, RW_STEPS, 0, True))

            @block.vector
            def _(dve):
                r.zero_dve(dve)
                run_steps(dve, RW_STEPS, r.dve)
                drain(r.dve(dve, RW_STEPS, 0, True))


class Readout:

    def __init__(self, nc, m, A, S, K):
        self.nc, self.A, self.S, self.K = nc, A, S, K
        sb, sem = m.sb, m.sem
        self.w_out, self.w_rt = sb("w_out", [P, KD, D]), sb("w_router", [P, KD, N_GRP + N_EXP])
        self.rows = {n: sb(n, [P, D]) for n in ("g1", "ln_g", "ln_b", "scale", "shift")}
        self.half = {n: sb(n, [P, D_HG]) for n in ("hg_w", "gn_w", "gn_b")}
        self.b_rt = sb("router_bias", [P, N_GRP + N_EXP])
        self.o = [sb(f"hg_o{d}", [P, D_HG]) for d in range(2)]
        self.y = [sb(f"rw_y{d}", [P, D_RW]) for d in range(2)]
        self.hg, self.rg, self.v, self.bo = sb("hg_g", [P, D_HG]), sb("rw_g", [P, D_RW]), sb("v", [P, D_RW]), sb("bonus", [P, RH])
        self.sq, self.sq2 = sb("squares", [P, D_HG]), sb("squares_rw", [P, D_RW])
        self.hs, self.hr = sb("hg_sum", [P, HH]), sb("hg_rstd", [P, HH])
        self.ys, self.yv, self.yr = sb("rw_mean", [P, RH]), sb("rw_var", [P, RH]), sb("rw_rstd", [P, RH])
        self.mix, self.mT = sb("mix", [P, D]), sb("mixT", [P, KD, P])
        self.x, self.z, self.h = sb("x", [P, D]), sb("z", [P, D]), sb("h", [P, D])
        self.hT = sb("hT", [P, KD, P])
        self.st, self.mv, self.rstd = sb("stats", [P, 2, 2, 6]), sb("mean_var", [P, 2, 2]), sb("rstd", [P, 2])
        self.lg, self.m8, self.i8 = sb("logits", [P, N_GRP + N_EXP]), sb("top8", [P, 8]), sb("top8_at", [P, 8], U32)
        self.e8, self.ei8 = sb("top8_in", [P, 8]), sb("top8_in_at", [P, 8], U32)
        self.gi, self.ng, self.ge, self.gs = sb("group", [P, 1]), sb("minus_max", [P, 1]), sb("group_exp", [P, 8]), sb("group_sum", [P, 1])
        self.oh, self.pick, self.el = sb("group_onehot", [P, 8]), sb("picked", [P, 8, 8]), sb("in_group", [P, 8])
        self.ei, self.dv, self.ex = sb("expert", [P, 2]), sb("diff", [P, 1]), sb("diff_exp", [P, 1])
        self.w2 = sb("weights", [P, 2])
        self.e1 = sb("expert_onehot", [P, 2, N_EXP])
        self.es, self.run, self.rk = sb("both", [P, N_EXP]), K["run"], sb("rank_terms", [P, 2, N_EXP])
        self.pt = [m.ps(f"turned{j}", [P, 512]) for j in range(2)]
        self.py = [m.ps(f"projected{j}", [P, 512]) for j in range(2)]
        self.ph = [m.ps(f"h_turned{j}", [P, 512]) for j in range(2)]
        self.pl, self.pc = m.ps("logits_psum", [P, 512]), m.ps("rank_psum", [P, 512])
        names = ("consts loaded x_loaded hg_sq hg_rstd_ready hg_part var_ready rw_rstd_ready mixed mix_turned mix_copied "
                 "projected residual stat1 rstd1 x1_ready x1_stored stat2 rstd2 h_ready h_stored h_turned h_copied logits_done "
                 "logits_ready neg_ready gexp dv_ready dexp onehot ranks order_dve order_pool order_c loads_used").split()
        self.s = {n: sem(n) for n in names}

    N_CONST = 16 * (2 + 2 + 5 + 3 + 2)

    def consts(self, sp):
        A, S, s = self.A, self.S, self.s
        c = s["consts"]
        sp.dma_start(self.w_out[:, 0:4], A["w_out"][0, 0:512].rearrange("(k p) n -> p k n", p=P)).then_inc(c, 16)
        sp.dma_start(self.w_out[:, 4:8], A["w_out"][0, 512:1024].rearrange("(k p) n -> p k n", p=P)).then_inc(c, 16)
        sp.dma_start(self.w_rt[:, :, 0:N_GRP], A["moe_w_group"][0].rearrange("(k p) n -> p k n", p=P)).then_inc(c, 16)
        sp.dma_start(self.w_rt[:, :, N_GRP:], A["moe_w_router"][0].rearrange("(k p) n -> p k n", p=P)).then_inc(c, 16)
        for t, src in ((self.rows["g1"], S["mod"][0, 2 * D:3 * D]), (self.rows["ln_g"], A["ln1_g"][0]), (self.rows["ln_b"], A["ln1_b"][0]),
                       (self.rows["scale"], S["mod"][0, 4 * D:5 * D]), (self.rows["shift"], S["mod"][0, 3 * D:4 * D]),
                       (self.half["hg_w"], A["hg_norm_w"][0]), (self.half["gn_w"], A["rw_gn_w"][0]), (self.half["gn_b"], A["rw_gn_b"][0])):
            sp.dma_start(t[:], src.partition_broadcast(P)).then_inc(c, 16)
        sp.dma_start(self.b_rt[:, 0:N_GRP], A["moe_b_group"][0].partition_broadcast(P)).then_inc(c, 16)
        sp.dma_start(self.b_rt[:, N_GRP:], A["moe_b_router"][0].rearrange("g e -> (g e)").partition_broadcast(P)).then_inc(c, 16)

    N_LOAD = 2 + 8 + 2 + 2 + 1

    def load(self, sp, i):
        S, s = self.S, self.s
        c = s["loaded"]
        wait(sp, s["mixed"], i)
        sp.sem_inc(s["loads_used"], 1)
        sp.dma_start(self.o[0][:], S["hg_o"][0, bass.ds(i + 2, 1)].rearrange("n p e -> p (n e)")).then_inc(c, 16)
        sp.dma_start(self.o[1][:], S["hg_o"][1, bass.ds((HG_STEPS - 1) - i, 1)].rearrange("n p e -> p (n e)")).then_inc(c, 16)
        for cc in range(2):
            q = slice(cc * RW_C, (cc + 1) * RW_C)
            for d, n in ((0, 2 * i + (4 + cc)), (1, (RW_STEPS - 1 - cc) - 2 * i)):
                src = S["rw_y"][d, bass.ds(n, 1)].rearrange("n (h t) j e -> h t (n j) e", h=2)
                dst = self.y[d][q].rearrange("t (j h e) -> t j h e", h=2, e=RW_C)
                for h in range(2):
                    sp.dma_start(dst[:, :, h, :], src[h]).then_inc(c, 16)
            sp.dma_start(self.v[q], S["rw_tm"][0, bass.ds(2 * i + (4 + cc), 1), :, 2, :].rearrange("n s e -> s (n e)")).then_inc(c, 16)
        sp.dma_start(self.hg[:], S["hg_g"][bass.ds(i * P + CTX, P), :]).then_inc(c, 16)
        sp.dma_start(self.rg[:], S["rw_g"][bass.ds(i * P + CTX, P), :]).then_inc(c, 16)
        sp.dma_start(self.bo[:], S["rw_bonus"][bass.ds(i * P + CTX, P), :]).then_inc(c, 16)

    def load_x(self, sp, i):
        wait(sp, self.s["residual"], i)
        sp.sem_inc(self.s["loads_used"], 1)
        sp.dma_start(self.x[:], self.A["x"][0, bass.ds(i * P, P), :]).then_inc(self.s["x_loaded"], 16)

    def pool_a(self, pool, i, o):
        G, s = self.nc.gpsimd, self.s
        pool.wait_ge(s["loaded"], 16 * self.N_LOAD * (i + 1))
        heads = lambda t: t[:].rearrange("p (h e) -> p h e", h=HH)
        wait(pool, s["mix_turned"], i)
        o.link(G.tensor_tensor(self.o[0][:], self.o[0][:], self.o[1][:], ALU.add))
        G.tensor_tensor(self.sq[:], self.o[0][:], self.o[0][:], ALU.mult).then_inc(s["hg_sq"], 1)
        pool.wait_ge(s["hg_rstd_ready"], i + 1)
        o.link(G.tensor_tensor(self.hr[:], self.hs[:], self.K["half"][:, 0:HH], ALU.pow))
        o.link(G.tensor_tensor(heads(self.o[0]), heads(self.o[0]), self.hr[:].unsqueeze(2).broadcast_to([P, HH, P]), ALU.mult))
        o.link(G.tensor_tensor(self.o[0][:], self.o[0][:], self.half["hg_w"][:], ALU.mult))
        G.tensor_tensor(self.mix[:, 0:D_HG], self.o[0][:], self.hg[:], ALU.mult).then_inc(s["hg_part"], 1)
        pool.wait_ge(s["var_ready"], i + 1)
        G.tensor_tensor(self.yr[:], self.yv[:], self.K["half"][:, 0:RH], ALU.pow).then_inc(s["rw_rstd_ready"], 1)

    def dve_a(self, dve, i, o):
        V, s = self.nc.vector, self.s
        y, sq = self.y[0], self.sq2
        dve.wait_ge(s["loaded"], 16 * self.N_LOAD * (i + 1))
        heads = lambda t: t[:].rearrange("p (h e) -> p h e", h=RH)
        bc = lambda t: t[:].unsqueeze(2).broadcast_to([P, RH, RW_C])
        o.link(V.tensor_tensor(y[:], y[:], self.y[1][:], ALU.add))
        o.link(V.tensor_reduce(self.ys[:], heads(y), AX.X, ALU.add))
        o.link(V.tensor_scalar(self.ys[:], self.ys[:], 1.0 / RW_C, None, ALU.mult))
        dve.wait_ge(s["hg_sq"], i + 1)
        o.link(V.tensor_reduce(self.hs[:], self.sq[:].rearrange("p (h e) -> p h e", h=HH), AX.X, ALU.add))
        V.tensor_scalar(self.hs[:], self.hs[:], 1.0 / P, HEAD_EPS, ALU.mult, ALU.add).then_inc(s["hg_rstd_ready"], 1)
        o.link(V.tensor_tensor(heads(y), heads(y), bc(self.ys), ALU.subtract))
        o.link(V.tensor_tensor(sq[:], y[:], y[:], ALU.mult))
        o.link(V.tensor_reduce(self.yv[:], heads(sq), AX.X, ALU.add))
        V.tensor_scalar(self.yv[:], self.yv[:], 1.0 / RW_C, GN_EPS, ALU.mult, ALU.add).then_inc(s["var_ready"], 1)
        o.link(V.tensor_tensor(heads(self.v), heads(self.v), bc(self.bo), ALU.mult))
        o.link(V.tensor_tensor(self.v[:], self.v[:], self.half["gn_b"][:], ALU.add))
        dve.wait_ge(s["rw_rstd_ready"], i + 1)
        o.link(V.tensor_tensor(heads(y), heads(y), bc(self.yr), ALU.mult))
        o.link(V.tensor_tensor(y[:], y[:], self.half["gn_w"][:], ALU.mult))
        o.link(V.tensor_tensor(y[:], y[:], self.v[:], ALU.add))
        wait(dve, s["mix_turned"], i)
        dve.wait_ge(s["hg_part"], i + 1)
        V.tensor_tensor(self.mix[:, D_HG:], y[:], self.rg[:], ALU.mult).then_inc(s["mixed"], 1)

    def norm(self, dve, o, src, i, k):
        V, s = self.nc.vector, self.s
        V.bn_stats(self.st[:, k, 0, :], src[:, 0:512])
        o.link(V.bn_stats(self.st[:, k, 1, :], src[:, 512:1024]))
        V.memset(self.K["spare"][:, k:k + 1], 0.0)
        o.link(V.bn_aggr(self.mv[:, k, :], self.st[:, k]))
        V.tensor_scalar(self.mv[:, k, 1:2], self.mv[:, k, 1:2], LN_EPS, None, ALU.add).then_inc(s[f"stat{k + 1}"], 1)
        dve.wait_ge(s[f"rstd{k + 1}"], i + 1)

    def dve_b(self, dve, i, o):
        V, s, R, K = self.nc.vector, self.s, self.rows, self.K
        z, h = self.z, self.h
        dve.wait_ge(s["projected"], i + 1)
        wait(dve, s["x1_stored"], 16 * i)
        for j in range(2):
            o.link(V.tensor_tensor(z[:, j * 512:(j + 1) * 512], self.py[j][:], R["g1"][:, j * 512:(j + 1) * 512], ALU.mult))
        dve.wait_ge(s["x_loaded"], 16 * (i + 1))
        o.link(V.scalar_tensor_tensor(z[:], self.x[:], ALPHA, z[:], ALU.mult, ALU.add))
        dve.sem_inc(s["residual"], 1)
        self.norm(dve, o, z, i, 0)
        o.link(V.tensor_scalar(z[:], z[:], self.mv[:, 0, 0:1], self.rstd[:, 0:1], ALU.subtract, ALU.mult))
        o.link(V.tensor_tensor(z[:], z[:], R["ln_g"][:], ALU.mult))
        o.link(V.tensor_tensor(z[:], z[:], R["ln_b"][:], ALU.add))
        dve.sem_inc(s["x1_ready"], 1)
        self.norm(dve, o, z, i, 1)
        wait(dve, s["h_stored"], 16 * i)
        wait(dve, s["h_turned"], i)
        o.link(V.tensor_scalar(h[:], z[:], self.mv[:, 1, 0:1], self.rstd[:, 1:2], ALU.subtract, ALU.mult))
        o.link(V.tensor_tensor(h[:], h[:], R["scale"][:], ALU.mult))
        V.tensor_tensor(h[:], h[:], R["shift"][:], ALU.add).then_inc(s["h_ready"], 1)
        dve.wait_ge(s["logits_done"], i + 1)
        lg, gl = self.lg, self.lg[:, 0:N_GRP]
        o.link(V.tensor_tensor(lg[:], self.pl[:, 0:N_GRP + N_EXP], self.b_rt[:], ALU.add))
        V.memset(K["spare"][:, 2:3], 0.0)
        o.link(V.max(self.m8[:], gl))
        V.tensor_scalar(self.ng[:], self.m8[:, 0:1], -1.0, None, ALU.mult).then_inc(s["neg_ready"], 1)
        o.link(V.max_index(self.i8[:], self.m8[:], gl))
        o.link(V.tensor_copy(self.gi[:], self.i8[:, 0:1]))
        o.link(V.tensor_scalar(self.oh[:], K["iota"][:, 0:8], self.gi[:, 0:1], None, ALU.is_equal))
        o.link(V.tensor_tensor(self.pick[:], lg[:, N_GRP:].rearrange("p (g e) -> p e g", g=N_GRP),
                               self.oh[:].unsqueeze(1).broadcast_to([P, 8, N_GRP]), ALU.mult))
        o.link(V.tensor_reduce(self.el[:], self.pick[:], AX.X, ALU.add))
        V.memset(K["spare"][:, 3:4], 0.0)
        o.link(V.max(self.e8[:], self.el[:]))
        V.tensor_tensor(self.dv[:], self.e8[:, 1:2], self.e8[:, 0:1], ALU.subtract).then_inc(s["dv_ready"], 1)
        o.link(V.max_index(self.ei8[:], self.e8[:], self.el[:]))
        o.link(V.tensor_copy(self.ei[:], self.ei8[:, 0:2]))
        o.link(V.scalar_tensor_tensor(self.ei[:], self.gi[:].broadcast_to([P, 2]), float(EPG), self.ei[:], ALU.mult, ALU.add))
        for j in range(2):
            o.link(V.tensor_scalar(self.e1[:, j, :], K["iota"][:, 0:N_EXP], self.ei[:, j:j + 1], None, ALU.is_equal))
        V.tensor_tensor(self.es[:], self.e1[:, 0, :], self.e1[:, 1, :], ALU.add).then_inc(s["onehot"], 1)
        V.tensor_copy(K["expert"][:, bass.ds(i * 2, 2)], self.ei[:])
        dve.wait_ge(s["gexp"], i + 1)
        o.link(V.reciprocal(self.gs[:], self.gs[:]))
        dve.wait_ge(s["dexp"], i + 1)
        o.link(V.tensor_scalar(self.dv[:], self.ex[:], 1.0, None, ALU.add))
        o.link(V.reciprocal(self.dv[:], self.dv[:]))
        o.link(V.tensor_tensor(self.w2[:, 0:1], self.dv[:], self.gs[:], ALU.mult))
        o.link(V.tensor_tensor(self.w2[:, 1:2], self.w2[:, 0:1], self.ex[:], ALU.mult))
        V.tensor_copy(K["weight"][:, bass.ds(i * 2, 2)], self.w2[:])
        dve.wait_ge(s["ranks"], i + 1)
        o.link(V.tensor_tensor(self.rk[:], self.e1[:], self.pc[:, 0:N_EXP].unsqueeze(1).broadcast_to([P, 2, N_EXP]), ALU.mult))
        o.link(V.tensor_reduce(self.w2[:], self.rk[:], AX.X, ALU.add))
        V.tensor_copy(K["rank"][:, bass.ds(i * 2, 2)], self.w2[:])
        o.link(V.tensor_tensor(self.run[:], self.run[:], self.es[:], ALU.add))

    def pool_b(self, pool, i):
        for k in range(2):
            pool.wait_ge(self.s[f"stat{k + 1}"], i + 1)
            self.nc.gpsimd.tensor_tensor(self.rstd[:, k:k + 1], self.mv[:, k, 1:2], self.K["half"][:, 0:1], ALU.pow).then_inc(self.s[f"rstd{k + 1}"], 1)

    def turn(self, pe, src, banks, dst_sem):
        for k in range(KD):
            t = self.nc.tensor.transpose(banks[k // 4][:, (k % 4) * P:(k % 4 + 1) * P], src[:, k * P:(k + 1) * P], self.K["ident"][:])
        t.then_inc(dst_sem, 1)

    def pe_a(self, pe, i):
        s = self.s
        pe.wait_ge(s["mixed"], i + 1)
        wait(pe, s["mix_copied"], 2 * i)
        self.turn(pe, self.mix, self.pt, s["mix_turned"])
        pe.wait_ge(s["mix_copied"], 2 * i + 2)
        wait(pe, s["residual"], i)
        for j in range(2):
            for k in range(KD):
                mm = self.nc.tensor.matmul(self.py[j][:], self.mT[:, k, :], self.w_out[:, k, j * 512:(j + 1) * 512], start=(k == 0), stop=(k == KD - 1))
        mm.then_inc(s["projected"], 1)

    def pe_b(self, pe, i):
        nc, s = self.nc, self.s
        pe.wait_ge(s["h_ready"], i + 1)
        wait(pe, s["h_copied"], 2 * i)
        self.turn(pe, self.h, self.ph, s["h_turned"])
        pe.wait_ge(s["h_copied"], 2 * i + 2)
        for k in range(KD):
            mm = nc.tensor.matmul(self.pl[:, 0:N_GRP + N_EXP], self.hT[:, k, :], self.w_rt[:, k, :], start=(k == 0), stop=(k == KD - 1))
        mm.then_inc(s["logits_done"], 1)
        pe.wait_ge(s["onehot"], i + 1)
        nc.tensor.matmul(self.pc[:, 0:N_EXP], self.K["lt"][:], self.es[:], start=True, stop=False)
        nc.tensor.matmul(self.pc[:, 0:N_EXP], self.K["ones"][:], self.run[:], start=False, stop=True).then_inc(s["ranks"], 1)

    def act_a(self, act, i):
        nc, s = self.nc, self.s
        act.wait_ge(s["mix_turned"], i + 1)
        wait(act, s["projected"], i)
        for j in range(2):
            nc.scalar.activation(self.mT[:, 4 * j:4 * j + 4, :].rearrange("p k t -> p (k t)"), self.pt[j][:], ACT.Copy).then_inc(s["mix_copied"], 1)

    def act_b(self, act, i):
        nc, s = self.nc, self.s
        act.wait_ge(s["x1_ready"], i + 1)
        act.dma_start(self.S["x1"][bass.ds(i * P, P), :], self.z[:]).then_inc(s["x1_stored"], 16)
        act.wait_ge(s["h_ready"], i + 1)
        act.dma_start(self.S["h2"][bass.ds(i * P, P), :], self.h[:]).then_inc(s["h_stored"], 16)
        act.wait_ge(s["h_turned"], i + 1)
        for j in range(2):
            nc.scalar.activation(self.hT[:, 4 * j:4 * j + 4, :].rearrange("p k t -> p (k t)"), self.ph[j][:], ACT.Copy).then_inc(s["h_copied"], 1)
        act.wait_ge(s["neg_ready"], i + 1)
        nc.scalar.activation(self.ge[:], self.lg[:, 0:N_GRP], ACT.Exp, bias=self.ng[:, 0:1], accum_out=self.gs[:]).then_inc(s["gexp"], 1)
        act.wait_ge(s["dv_ready"], i + 1)
        nc.scalar.activation(self.ex[:], self.dv[:], ACT.Exp).then_inc(s["dexp"], 1)


EPG = N_EXP // N_GRP


def readout(nc, A, S, K):
    with ExitStack() as ctx:
        m = Mem(nc, ctx, "read")
        r = Readout(nc, m, A, S, K)
        s = r.s

        def pipeline(eng, a, b):
            a(0)
            a(1)
            b(0)
            with eng.Fori(2, N_TILES) as i:
                a(i)
                b(i - 1)
            b(N_TILES - 1)

        with nc.Block() as block:
            @block.sync
            def _(sp):
                r.consts(sp)
                r.load(sp, 0)
                r.load_x(sp, 0)
                with sp.Fori(1, N_TILES) as i:
                    r.load(sp, i)
                    r.load_x(sp, i)

            @block.gpsimd
            def _(pool):
                pool.wait_ge(s["consts"], r.N_CONST)
                o = Order(pool, s["order_pool"])
                ordered_pipeline(pool, [o], lambda i: r.pool_a(pool, i, o), lambda i: r.pool_b(pool, i))

            @block.scalar
            def _(act):
                pipeline(act, lambda i: r.act_a(act, i), lambda i: r.act_b(act, i))
                act.wait_ge(s["x1_stored"], 16 * N_TILES)
                act.wait_ge(s["h_stored"], 16 * N_TILES)

            @block.tensor
            def _(pe):
                pe.wait_ge(s["consts"], r.N_CONST)
                pipeline(pe, lambda i: r.pe_a(pe, i), lambda i: r.pe_b(pe, i))

            @block.vector
            def _(dve):
                oa, ob, oc = Order(dve, s["order_dve"]), Order(dve, m.sem("order_residual")), Order(dve, s["order_c"])
                dve.wait_ge(s["consts"], r.N_CONST)
                oc.link(nc.vector.memset(r.run[:], 0.0))
                oc.link(nc.vector.tensor_scalar(r.rows["scale"][:], r.rows["scale"][:], 1.0, None, ALU.add))
                ordered_pipeline(dve, [oa, ob], lambda i: r.dve_a(dve, i, oa), lambda i: r.dve_b(dve, i, ob))


def ordered_pipeline(eng, orders, a, b):
    def run(f, o, i, k0=0):
        o.g, o.k = i, 0
        f(i)
        if isinstance(i, int) and i == 0:
            o.per = o.k
        assert o.k == o.per or o.k == 0
    ob = orders[-1] if len(orders) > 1 else Order(eng, None)
    run(a, orders[0], 0)
    run(a, orders[0], 1)
    run(b, ob, 0)
    with eng.Fori(2, N_TILES) as i:
        run(a, orders[0], i)
        run(b, ob, i - 1)
    run(b, ob, N_TILES - 1)


def dispatch(nc, A, S, K):
    with ExitStack() as ctx:
        m = Mem(nc, ctx, "disp")
        cnt, nblk, incl, start = (m.sb(x, [P, N_EXP]) for x in ("counts", "blocks", "blocks_sum", "starts"))
        onehot = m.sb("onehot", [P, 2 * N_TILES, N_EXP])
        place = m.sb("place", [P, 2 * N_TILES])
        pair = m.sb("token_slot", [P, N_TILES, 2, 2], I32)
        cmp = m.sb("compare", [P, MAX_BLOCKS + 2, N_EXP])
        be = m.sb("block_expert", [P, MAX_BLOCKS + 2])
        pairs = m.sb("pairs", [P, 1])
        ps = m.ps("counts_psum", [P, 512])
        vo, cd, pd, td, sd = (m.sem(x) for x in ("dve_order", "counts_done", "places_ready", "tokens_ready", "scattered"))
        with nc.Block() as block:
            @block.tensor
            def _(pe):
                nc.tensor.matmul(ps[:, 0:N_EXP], K["ones"][:], K["run"][:], start=True, stop=True).then_inc(cd, 1)

            @block.vector
            def _(dve):
                V, o = nc.vector, Order(dve, vo)
                dve.wait_ge(cd, 1)
                o.link(V.tensor_copy(cnt[:], ps[:, 0:N_EXP]))
                o.link(V.memset(nblk[:], 0.0))
                for b in range(LAT // BLK):
                    o.link(V.scalar_tensor_tensor(nblk[:], cnt[:], float(b * BLK), nblk[:], ALU.is_gt, ALU.add))
                o.link(V.tensor_tensor_scan(incl[:], K["one"][:].broadcast_to([P, N_EXP]), nblk[:], 0.0, ALU.mult, ALU.add))
                o.link(V.tensor_tensor(start[:], incl[:], nblk[:], ALU.subtract))
                o.link(V.tensor_scalar(start[:], start[:], float(BLK), None, ALU.mult))
                o.link(V.tensor_tensor(onehot[:], K["iota"][:, 0:N_EXP].unsqueeze(1).broadcast_to([P, 2 * N_TILES, N_EXP]),
                                       K["expert"][:].unsqueeze(2).broadcast_to([P, 2 * N_TILES, N_EXP]), ALU.is_equal))
                o.link(V.tensor_tensor(onehot[:], onehot[:], start[:].unsqueeze(1).broadcast_to([P, 2 * N_TILES, N_EXP]), ALU.mult))
                o.link(V.tensor_reduce(place[:], onehot[:], AX.X, ALU.add))
                V.tensor_tensor(K["place"][:, 0:2 * N_TILES], place[:], K["rank"][:], ALU.add).then_inc(pd, 1)
                nb = MAX_BLOCKS + 2
                o.link(V.tensor_tensor(cmp[:], incl[:].unsqueeze(1).broadcast_to([P, nb, N_EXP]),
                                       K["iota"][:, 0:nb].unsqueeze(2).broadcast_to([P, nb, N_EXP]), ALU.is_le))
                o.link(V.tensor_reduce(be[:], cmp[:], AX.X, ALU.add))
                o.link(V.tensor_scalar(K["block_expert"][:], be[:], float(N_EXP - 1), None, ALU.min))
                o.link(V.tensor_scalar(pairs[:], incl[:, N_EXP - 1:N_EXP], 0.5, 0.25, ALU.mult, ALU.add))
                o.link(V.tensor_copy(K["pairs"][:], pairs[:]))

            @block.gpsimd
            def _(pool):
                for j in range(2):
                    nc.gpsimd.iota(pair[:, :, j, 0], pattern=[[P, N_TILES]], base=0, channel_multiplier=1)
                    nc.gpsimd.iota(pair[:, :, j, 1], pattern=[[2 * P, N_TILES]], base=j, channel_multiplier=2).then_inc(td, 1)
                pool.wait_ge(td, 2)
                pool.wait_ge(pd, 1)
                for t in range(N_TILES):
                    for j in range(2):
                        pool.indirect_dma_start(out=S["row_list"], out_offset=bass.IndirectOffsetOnAxis(ap=K["place"][:, 2 * t + j:2 * t + j + 1], axis=0),
                                                in_=pair[:, t, j, :], in_offset=None).then_inc(sd, 16)
                pool.wait_ge(sd, 16 * 2 * N_TILES)


def experts(nc, A, S, K):
    KF = D_EXP // P
    with ExitStack() as ctx:
        m = Mem(nc, ctx, "exp")
        two = lambda name, shape, dt=F32: [m.sb(f"{name}{u}", shape, dt) for u in range(2)]
        wg, wu, wd = two("w_gate", [P, KD, D_EXP]), two("w_up", [P, KD, D_EXP]), two("w_down", [P, KF, D])
        tok, slot = two("row_token", [P, 1], I32), two("row_slot", [P, 1], I32)
        xb, xT = two("rows", [P, D]), two("rowsT", [P, KD, P])
        act_, hid, hT, yb = two("silu", [P, D_EXP]), two("hidden", [P, D_EXP]), two("hiddenT", [P, KF, P]), two("out", [P, D])
        px = [m.ps(f"rows_turned{j}", [P, 512]) for j in range(2)]
        pg, pu, ph = m.ps("gate", [P, 512]), m.ps("up", [P, 512]), m.ps("hidden_turned", [P, 512])
        pd = [m.ps(f"down{j}", [P, 512]) for j in range(2)]
        names = ("x_turned xT_ready gate_done up_done silu_ready hid_ready h_turned hT_ready down_done out_ready0 out_ready1 turns").split()
        s = {n: m.sem(n) for n in names}
        ld = {n: [m.sem(f"{n}{u}") for u in range(2)] for n in ("tok", "slot", "rows", "gate", "up", "down", "stored")}
        load_n = lambda eng: eng.value_load(K["pairs"][0:1, 0:1], min_val=1, max_val=MAX_BLOCKS // 2)

        def turns(eng, body):
            n = load_n(eng)
            for u in range(2):
                body(u, u)
            with eng.Fori(1, n) as g:
                for u in range(2):
                    body(2 * g + u, u)
            return n

        with nc.Block() as block:
            @block.sync
            def _(sp):
                def body(b, u):
                    e = sp.value_load(K["block_expert"][0:1, bass.ds(b, 1)], min_val=0, max_val=N_EXP - 1)
                    for name, w, buf, done in (("gate", "moe_w_gate", wg, "gate_done"), ("up", "moe_w_up", wu, "up_done"),
                                               ("down", "moe_w_down", wd, "down_done")):
                        wait(sp, s[done], b - 1)
                        sp.dma_start(buf[u][:], A[w][0, bass.ds(e, 1)].rearrange("o (p k) f -> p (o k) f", p=P)).then_inc(ld[name][u], 16)
                turns(sp, body)

            @block.gpsimd
            def _(pool):
                def list_part(b, u, buf, j, name):
                    pool.sem_inc(s["turns"], 1)
                    pool.dma_start(buf[u][:], S["row_list"][bass.ds(b * BLK, BLK), j:j + 1]).then_inc(ld[name][u], 16)

                def gather(b, u):
                    pool.wait_ge(ld["tok"][u], 8 * (b - u) + 16)
                    pool.sem_inc(s["turns"], 1)
                    pool.indirect_dma_start(out=xb[u][:], out_offset=None, in_=S["h2"],
                                            in_offset=bass.IndirectOffsetOnAxis(ap=tok[u][:, 0:1], axis=0)).then_inc(ld["rows"][u], 16)

                def body(b, u):
                    wait(pool, ld["stored"][u], 8 * (b - u))
                    list_part(b, u, slot, 1, "slot")
                    pool.wait_ge(s["x_turned"], b + 1)
                    list_part(b + 2, u, tok, 0, "tok")
                    gather(b + 2, u)
                    pool.wait_ge(s["out_ready0"], b + 1)
                    pool.wait_ge(s["out_ready1"], b + 1)
                    pool.wait_ge(ld["slot"][u], 8 * (b - u) + 16)
                    pool.sem_inc(s["turns"], 1)
                    pool.indirect_dma_start(out=S["yb"], out_offset=bass.IndirectOffsetOnAxis(ap=slot[u][:, 0:1], axis=0),
                                            in_=yb[u][:], in_offset=None).then_inc(ld["stored"][u], 16)

                for b in range(2):
                    list_part(b, b, tok, 0, "tok")
                for b in range(2):
                    gather(b, b)
                n = turns(pool, body)
                for u in range(2):
                    pool.wait_ge(ld["stored"][u], n * 16)
                    pool.wait_ge(ld["rows"][u], n * 16 + 16)
                pool.sem_inc(s["turns"], 1)

            @block.scalar
            def _(act):
                def body(b, u):
                    act.wait_ge(s["gate_done"], b + 1)
                    wait(act, s["hid_ready"], b - 1)
                    nc.scalar.activation(act_[u][:], pg[:], ACT.Silu).then_inc(s["silu_ready"], 1)
                    act.wait_ge(s["h_turned"], b + 1)
                    wait(act, s["down_done"], b - 1)
                    nc.scalar.activation(hT[u][:].rearrange("p k t -> p (k t)"), ph[:], ACT.Copy).then_inc(s["hT_ready"], 1)
                    act.wait_ge(s["down_done"], b + 1)
                    wait(act, ld["stored"][u], 8 * (b - u))
                    nc.scalar.activation(yb[u][:, 0:512], pd[0][:], ACT.Copy).then_inc(s["out_ready0"], 1)
                turns(act, body)

            @block.vector
            def _(dve):
                def rows(b, u):
                    dve.wait_ge(s["x_turned"], b + 1)
                    wait(dve, s["up_done"], b - 1)
                    for j in range(2):
                        i = nc.vector.tensor_copy(xT[u][:, 4 * j:4 * j + 4, :].rearrange("p k t -> p (k t)"), px[j][:])
                    i.then_inc(s["xT_ready"], 1)

                def body(b, u):
                    dve.wait_ge(s["up_done"], b + 1)
                    dve.wait_ge(s["silu_ready"], b + 1)
                    wait(dve, s["h_turned"], b - 1)
                    nc.vector.tensor_tensor(hid[u][:], act_[u][:], pu[:], ALU.mult).then_inc(s["hid_ready"], 1)
                    rows(b + 1, 1 - u)
                    dve.wait_ge(s["down_done"], b + 1)
                    wait(dve, ld["stored"][u], 8 * (b - u))
                    nc.vector.tensor_copy(yb[u][:, 512:1024], pd[1][:]).then_inc(s["out_ready1"], 1)
                rows(0, 0)
                turns(dve, body)

            @block.tensor
            def _(pe):
                def rows(b, u):
                    pe.wait_ge(ld["rows"][u], 8 * (b - u) + 16)
                    wait(pe, s["xT_ready"], b)
                    v = xb[u][:].rearrange("t (p k) -> t k p", k=KD)
                    for k in range(KD):
                        t = nc.tensor.transpose(px[k // 4][:, (k % 4) * P:(k % 4 + 1) * P], v[:, k, :], K["ident"][:])
                    t.then_inc(s["x_turned"], 1)

                def body(b, u):
                    pe.wait_ge(s["xT_ready"], b + 1)
                    wait(pe, s["silu_ready"], b)
                    wait(pe, s["hid_ready"], b)
                    for name, ps, w in (("gate", pg, wg), ("up", pu, wu)):
                        pe.wait_ge(ld[name][u], 8 * (b - u) + 16)
                        for k in range(KD):
                            mm = nc.tensor.matmul(ps[:], xT[u][:, k, :], w[u][:, k, :], start=(k == 0), stop=(k == KD - 1))
                        mm.then_inc(s[name + "_done"], 1)
                    rows(b + 1, 1 - u)
                    pe.wait_ge(s["hid_ready"], b + 1)
                    wait(pe, s["hT_ready"], b)
                    v = hid[u][:].rearrange("t (p k) -> t k p", k=KF)
                    for k in range(KF):
                        t = nc.tensor.transpose(ph[:, k * P:(k + 1) * P], v[:, k, :], K["ident"][:])
                    t.then_inc(s["h_turned"], 1)
                    pe.wait_ge(s["hT_ready"], b + 1)
                    pe.wait_ge(ld["down"][u], 8 * (b - u) + 16)
                    wait(pe, s["out_ready0"], b)
                    wait(pe, s["out_ready1"], b)
                    for j in range(2):
                        for k in range(KF):
                            mm = nc.tensor.matmul(pd[j][:], hT[u][:, k, :], wd[u][:, k, j * 512:(j + 1) * 512], start=(k == 0), stop=(k == KF - 1))
                    mm.then_inc(s["down_done"], 1)
                rows(0, 0)
                turns(pe, body)


def combine(nc, A, S, K):
    with ExitStack() as ctx:
        m = Mem(nc, ctx, "comb")
        g2, lg, lb = (m.sb(x, [P, D]) for x in ("g2", "ln_g", "ln_b"))
        w = [m.sb(f"weight{u}", [P, 2]) for u in range(2)]
        y = [m.sb(f"y{u}", [P, 2, D]) for u in range(2)]
        x = [m.sb(f"x{u}", [P, D]) for u in range(2)]
        st, mv, rstd = m.sb("stats", [P, 2, 2, 6]), m.sb("mean_var", [P, 2, 2]), m.sb("rstd", [P, 2])
        names = "consts stat rstd ready order turns".split()
        s = {n: m.sem(n) for n in names}
        ld = {n: [m.sem(f"{n}{u}") for u in range(2)] for n in ("x", "stored")}

        def tiles(eng, body):
            for u in range(2):
                body(u, u)
            with eng.Fori(1, N_TILES // 2) as g:
                for u in range(2):
                    body(2 * g + u, u)

        with nc.Block() as block:
            @block.sync
            def _(sp):
                for t, src in ((g2, S["mod"][0, 5 * D:6 * D]), (lg, A["ln2_g"][0]), (lb, A["ln2_b"][0])):
                    sp.dma_start(t[:], src.partition_broadcast(P)).then_inc(s["consts"], 16)

                def body(i, u):
                    wait(sp, ld["stored"][u], 8 * (i - u))
                    sp.sem_inc(s["turns"], 1)
                    sp.dma_start(x[u][:], S["x1"][bass.ds(i * P, P), :]).then_inc(ld["x"][u], 16)
                    sp.dma_start(y[u][:], S["yb"][bass.ds(i * 2 * P, 2 * P), :].rearrange("(p j) e -> p j e", j=2)).then_inc(ld["x"][u], 16)
                tiles(sp, body)

            @block.gpsimd
            def _(pool):
                def body(i, u):
                    pool.wait_ge(s["stat"], i + 1)
                    nc.gpsimd.tensor_tensor(rstd[:, u:u + 1], mv[:, u, 1:2], K["half"][:, 0:1], ALU.pow).then_inc(s["rstd"], 1)
                tiles(pool, body)

            @block.scalar
            def _(act):
                def body(i, u):
                    act.wait_ge(s["ready"], i + 1)
                    act.dma_start(K["out"][0, bass.ds(i * P, P), :], x[u][:]).then_inc(ld["stored"][u], 16)
                tiles(act, body)
                for u in range(2):
                    act.wait_ge(ld["stored"][u], 8 * N_TILES)

            @block.vector
            def _(dve):
                V, o = nc.vector, Order(dve, s["order"])

                def body(i, u):
                    o.link(V.tensor_copy(w[u][:], K["weight"][:, bass.ds(i * 2, 2)]))
                    dve.wait_ge(ld["x"][u], 16 * (i - u) + 32)
                    o.link(V.tensor_scalar(y[u][:, 0], y[u][:, 0], w[u][:, 0:1], None, ALU.mult))
                    o.link(V.scalar_tensor_tensor(y[u][:, 0], y[u][:, 1], w[u][:, 1:2], y[u][:, 0], ALU.mult, ALU.add))
                    o.link(V.tensor_tensor(y[u][:, 0], y[u][:, 0], g2[:], ALU.mult))
                    o.link(V.scalar_tensor_tensor(x[u][:], x[u][:], ALPHA, y[u][:, 0], ALU.mult, ALU.add))
                    V.bn_stats(st[:, u, 0, :], x[u][:, 0:512])
                    o.link(V.bn_stats(st[:, u, 1, :], x[u][:, 512:1024]))
                    V.memset(K["spare"][:, u:u + 1], 0.0)
                    o.link(V.bn_aggr(mv[:, u, :], st[:, u]))
                    V.tensor_scalar(mv[:, u, 1:2], mv[:, u, 1:2], LN_EPS, None, ALU.add).then_inc(s["stat"], 1)
                    dve.wait_ge(s["rstd"], i + 1)
                    o.link(V.tensor_scalar(x[u][:], x[u][:], mv[:, u, 0:1], rstd[:, u:u + 1], ALU.subtract, ALU.mult))
                    o.link(V.tensor_tensor(x[u][:], x[u][:], lg[:], ALU.mult))
                    V.tensor_tensor(x[u][:], x[u][:], lb[:], ALU.add).then_inc(s["ready"], 1)

                dve.wait_ge(s["consts"], 48)
                n0 = o.k

                def turn(g):
                    for u in range(2):
                        body(2 * g + u, u)
                turn(0)
                o.per = o.k - n0
                with dve.Fori(1, N_TILES // 2) as g:
                    o.g, o.k = g, n0
                    turn(g)
                    assert o.k == n0 + o.per

            @block.tensor
            def _(pe):
                pass


def scratch(nc, kind=None):
    kw = {} if kind is None else {"kind": kind}

    def t(name, shape, dt=F32):
        return nc.dram_tensor(f"s_{name}", shape, dt, **kw).ap()

    return {
        "mod": t("mod", (2, 6 * D)),
        "hg_in": t("hg_in", (2, HG_STEPS, 3, P, HH, P)),
        "hg_v": t("hg_v", (2, HG_STEPS, P, D_HG)),
        "hg_g": t("hg_g", (CTX + LAT, D_HG)),
        "rw_lat": t("rw_lat", (14, P, LAT + 2 * GRID_W)),
        "rw_ctx": t("rw_ctx", (14, P, CTX + 2)),
        "hg_o": t("hg_o", (2, HG_STEPS, P, D_HG)),
        "rw_in": t("rw_in", (2, RW_STEPS, P, ROW)),
        "rw_tm": t("rw_tm", (2, RW_STEPS, RW_C, 3, D_RW)),
        "rw_y": t("rw_y", (2, RW_STEPS, P, NPAIR, RW_C)),
        "rw_g": t("rw_g", (CTX + LAT, D_RW)),
        "rw_bonus": t("rw_bonus", (CTX + LAT, RH)),
        "x1": t("x1", (LAT, D)),
        "h2": t("h2", (LAT, D)),
        "row_list": t("row_list", ((MAX_BLOCKS + 2) * BLK, 2), I32),
        "yb": t("yb", (2 * LAT + 1, D)),
    }


def constants(nc, ctx):
    def sb(name, shape, dt=F32):
        return ctx.enter_context(nc.sbuf_tensor(f"const_{name}", shape, dt))

    return {"ident": sb("ident", [P, P]), "ones": sb("ones", [P, P]), "half": sb("minus_half", [P, 32]),
            "lb": sb("lb", [P, 2, HH]), "omlb": sb("one_minus_lb", [P, 2, HH]), "spare": sb("spare", [P, 32])}


def later_constants(nc, ctx):
    def sb(name, shape, dt=F32):
        return ctx.enter_context(nc.sbuf_tensor(f"const_{name}", shape, dt))

    return {"lvl": sb("level_masks", [P, 2, 7, P]), "before": sb("before_mask", [P, 2, P]), "upto": sb("upto_mask", [P, 2, P]),
            "first": sb("chunk_starts", [P, 2, HH, P]), "first64": sb("chunk64_starts", [P, 2, NPAIR * 4, RW_C]),
            "one": sb("one", [P, 1]), "eps": sb("eps", [P, 1]), "lt": sb("earlier_tokens", [P, P]), "iota": sb("iota", [P, MAX_BLOCKS + 2]),
            "run": sb("counts_so_far", [P, N_EXP]), "expert": sb("experts", [P, 2 * N_TILES]), "rank": sb("ranks", [P, 2 * N_TILES]),
            "weight": sb("weights", [P, 2 * N_TILES + 2]), "place": sb("places", [P, 2 * N_TILES + 2], U32),
            "block_expert": sb("block_experts", [P, MAX_BLOCKS + 2], I32), "pairs": sb("block_pairs", [P, 1], I32)}


def program(nc, A, out, S, stages=None):
    with ExitStack() as ctx:
        K = constants(nc, ctx)
        K["out"] = out
        with nc.allow_non_contiguous_dma(reason="vectors of a few KB laid out as columns"):
            for f in STAGES[:stages]:
                if f is masks:
                    K.update(later_constants(nc, ctx))
                f(nc, A, S, K)


STAGES = [modulation, projection, masks, rwkv_prep, hgrn_scan, rwkv_scan, readout, dispatch, experts, combine]

INPUTS = ("x c ctx c_ctx w_mod b_mod w_in w_out hg_lb_logits hg_norm_w rw_mu rw_w0 rw_w_decay2 rw_a0 rw_w_a2 rw_w_g2 "
          "rw_k_k rw_k_a rw_r_k rw_gn_w rw_gn_b ln1_g ln1_b ln2_g ln2_b moe_w_group moe_b_group moe_w_router "
          "moe_b_router moe_w_gate moe_w_up moe_w_down").split()


def kernel(**inputs):
    import numpy as np
    import concourse.bacc as bacc
    from concourse.bass_utils import run_bass_kernel_spmd

    nc = bacc.Bacc("TRN2", target_bir_lowering=False, num_devices=1)
    arrays, A = {}, {}
    for name in INPUTS:
        arrays[f"in_{name}_dram"] = np.ascontiguousarray(inputs[name])
        A[name] = nc.dram_tensor(f"in_{name}_dram", arrays[f"in_{name}_dram"].shape, F32, kind="ExternalInput").ap()
    out = nc.dram_tensor("out_dram", (1, LAT, D), F32, kind="ExternalOutput").ap()
    program(nc, A, out, scratch(nc))
    return run_bass_kernel_spmd(nc, [arrays], core_ids=[0]).results[0]["out_dram"]
```
